# Optimizing a Trainium2 kernel written in Bass

```python
import jax, jax.numpy as jnp
from jax import lax
import numpy as np

D_MODEL = 1024
BATCH = 1
SEQ = 256
DEPTH = 2

GRID_W = 64
N_MEM = 256
HEAD_DIM = 64
N_MIX_HEADS = D_MODEL // HEAD_DIM
ML_HEADS = (3 * N_MIX_HEADS) // 8
NA_HEADS = (N_MIX_HEADS - ML_HEADS) // 2
GLA_HEADS = N_MIX_HEADS - ML_HEADS - NA_HEADS
ML_DIM = ML_HEADS * HEAD_DIM
NA_DIM = NA_HEADS * HEAD_DIM
GLA_DK = HEAD_DIM // 2
GLA_KDIM = GLA_HEADS * GLA_DK
GLA_VDIM = GLA_HEADS * HEAD_DIM
D_MIX = ML_DIM + NA_DIM + GLA_VDIM
GLA_RANK = 16
GLA_TAU = 16.0
NA_KH_MAX = 8
NA_KW = 16
ML_CHUNK = 128
GLA_CHUNK = 64
X_HEADS = 4
X_HEAD_DIM = D_MODEL // X_HEADS
D_FF = ((8 * D_MODEL // 3 + 127) // 128) * 128
EPS = 1e-6
IN_SIZES = (ML_DIM, ML_DIM, ML_DIM, ML_DIM, 4 * ML_HEADS,
            NA_DIM, NA_DIM, NA_DIM,
            GLA_KDIM, GLA_KDIM, GLA_VDIM, GLA_VDIM, 2 * GLA_RANK)
IN_COLS = sum(IN_SIZES)

kernel_name = 'hybrid_mlstm_natten_gla_encoder'

def rms_norm(x, g):
    xf = x.astype(jnp.float32)
    y = xf * lax.rsqrt(jnp.mean(xf * xf, axis=-1, keepdims=True) + EPS)
    return (y * g.astype(jnp.float32)).astype(x.dtype)

def head_rms_norm(h, g, n_heads):
    B, T, C = h.shape
    hh = h.reshape(B, T, n_heads, C // n_heads)
    hh = hh * lax.rsqrt(jnp.mean(hh * hh, axis=-1, keepdims=True) + EPS)
    return hh.reshape(B, T, C) * g.astype(jnp.float32)

def dwconv_centred(x, w, b):
    xp = jnp.pad(x, ((0, 0), (1, 1), (0, 0)))
    return xp[:, :-2] * w[0] + xp[:, 1:-1] * w[1] + xp[:, 2:] * w[2] + b

def to_chunks(a, L):
    B, H, T = a.shape[:3]
    return jnp.moveaxis(a.reshape((B, H, T // L, L) + a.shape[3:]), 2, 0)

def from_chunks(a):
    a = jnp.moveaxis(a, 0, 2)
    return a.reshape(a.shape[:2] + (-1,) + a.shape[4:])

def mlstm_chunkwise(q, k, v, i_pre, f_pre):
    B, H, T, d = q.shape
    L = ML_CHUNK
    logf = jax.nn.log_sigmoid(f_pre)
    xs = tuple(to_chunks(a, L) for a in (q, k, v, i_pre, logf))
    causal = jnp.tril(jnp.ones((L, L), dtype=bool))

    def step(carry, inp):
        C, n, m = carry
        qb, kb, vb, ib, fb = inp
        b = jnp.cumsum(fb, axis=-1)
        g = b[..., -1]
        D = b[..., :, None] - b[..., None, :] + ib[..., None, :]
        D = jnp.where(causal, D, -jnp.inf)
        inter = b + m[..., None]
        m_row = jnp.maximum(inter, jnp.max(D, axis=-1))
        w_inter = jnp.exp(inter - m_row)
        s = jnp.einsum('bhid,bhjd->bhij', qb, kb) * jnp.exp(D - m_row[..., None])
        num = jnp.einsum('bhij,bhje->bhie', s, vb) + w_inter[..., None] * jnp.einsum('bhid,bhde->bhie', qb, C)
        den = jnp.sum(s, axis=-1) + w_inter * jnp.einsum('bhid,bhd->bhi', qb, n)
        h = num / jnp.maximum(jnp.abs(den), jnp.exp(-m_row))[..., None]
        tail = g[..., None] - b + ib
        m_new = jnp.maximum(g + m, jnp.max(tail, axis=-1))
        wk = jnp.exp(tail - m_new[..., None])
        decay = jnp.exp(g + m - m_new)
        C_new = decay[..., None, None] * C + jnp.einsum('bhj,bhjd,bhje->bhde', wk, kb, vb)
        n_new = decay[..., None] * n + jnp.einsum('bhj,bhjd->bhd', wk, kb)
        return (C_new, n_new, m_new), h

    init = (jnp.zeros((B, H, d, d), jnp.float32), jnp.zeros((B, H, d), jnp.float32), jnp.zeros((B, H), jnp.float32))
    _, hs = lax.scan(step, init, xs)
    return from_chunks(hs)

def gla_chunked(q, k, v, log_a):
    B, H, T, dk = q.shape
    dv = v.shape[-1]
    L = GLA_CHUNK
    xs = tuple(to_chunks(a, L) for a in (q, k, v, log_a))
    causal = jnp.tril(jnp.ones((L, L), dtype=bool))

    def step(S, inp):
        qb, kb, vb, ab = inp
        Bc = jnp.cumsum(ab, axis=2)
        Btot = Bc[:, :, -1]
        q_dec = qb * jnp.exp(Bc)
        A = jnp.einsum('bhid,bhjd->bhij', q_dec, kb * jnp.exp(-Bc))
        A = jnp.where(causal, A, 0.0)
        o = jnp.einsum('bhij,bhje->bhie', A, vb) + jnp.einsum('bhid,bhde->bhie', q_dec, S)
        k_tail = kb * jnp.exp(Btot[:, :, None, :] - Bc)
        S_new = jnp.exp(Btot)[..., None] * S + jnp.einsum('bhjd,bhje->bhde', k_tail, vb)
        return S_new, o

    _, os_ = lax.scan(step, jnp.zeros((B, H, dk, dv), jnp.float32), xs)
    return from_chunks(os_)

def neighbourhood_attention(q, k, v, rpb):
    B, T, H, d = q.shape
    rows = T // GRID_W
    kh = min(NA_KH_MAX, rows)
    qg = q.reshape(B, rows, GRID_W, H, d)
    kg = k.reshape(B, rows, GRID_W, H, d)
    vg = v.reshape(B, rows, GRID_W, H, d)
    r = jnp.arange(rows)
    row_start = jnp.clip(r - kh // 2, 0, rows - kh)
    key_rows = row_start[:, None] + jnp.arange(kh)[None, :]
    k_band = jnp.take(kg, key_rows, axis=1)
    v_band = jnp.take(vg, key_rows, axis=1)
    c = jnp.arange(GRID_W)
    col_start = jnp.clip(c - NA_KW // 2, 0, GRID_W - NA_KW)
    in_win = (c[None, :] >= col_start[:, None]) & (c[None, :] < col_start[:, None] + NA_KW)
    dr = key_rows - r[:, None] + (NA_KH_MAX - 1)
    dc = jnp.clip(c[None, :] - c[:, None], -(NA_KW - 1), NA_KW - 1) + (NA_KW - 1)
    bias = rpb.astype(jnp.float32)[:, dr[:, None, :, None], dc[None, :, None, :]]
    s = jnp.einsum('brqhd,brkwhd->bhrqkw', qg, k_band).astype(jnp.float32) * (d ** -0.5) + bias
    s = jnp.where(in_win[:, None, :], s, -jnp.inf)
    p = jax.nn.softmax(s.reshape(B, H, rows, GRID_W, kh * GRID_W), axis=-1).reshape(s.shape)
    o = jnp.einsum('bhrqkw,brkwhd->brqhd', p.astype(v.dtype), v_band)
    return o.reshape(B, T, H * d)

def hybrid_mixer(h, w_in, ml_conv_w, ml_conv_b, ml_gate_b, ml_norm_g, na_rpb,
                 gla_a_w2, gla_a_b, gla_norm_g, w_out):
    B, T, _ = h.shape
    f32 = jnp.float32
    proj = h @ w_in
    pts = []
    acc = 0
    for s_ in IN_SIZES[:-1]:
        acc += s_
        pts.append(acc)
    (ml_q, ml_k, ml_v, ml_o, ml_g, na_q, na_k, na_v,
     g_q, g_k, g_v, g_g, g_a) = jnp.split(proj, pts, axis=-1)

    def heads(a, n):
        return a.reshape(B, T, n, -1).transpose(0, 2, 1, 3).astype(f32)

    def flip(a):
        return jnp.flip(a, axis=2)

    qk = jax.nn.silu(dwconv_centred(jnp.concatenate([ml_q, ml_k], axis=-1), ml_conv_w, ml_conv_b))
    mq = heads(qk[..., :ML_DIM], ML_HEADS)
    mk = heads(qk[..., ML_DIM:], ML_HEADS) * (HEAD_DIM ** -0.5)
    mv = heads(ml_v, ML_HEADS)
    gates = ml_g.reshape(B, T, 4, ML_HEADS).astype(f32) + ml_gate_b.astype(f32)
    gates = gates.transpose(2, 0, 3, 1)
    h_f = mlstm_chunkwise(mq, mk, mv, gates[0], gates[1])
    h_b = flip(mlstm_chunkwise(flip(mq), flip(mk), flip(mv), flip(gates[2]), flip(gates[3])))
    ml_h = (h_f + h_b).transpose(0, 2, 1, 3).reshape(B, T, ML_DIM)
    ml_out = head_rms_norm(ml_h, ml_norm_g, ML_HEADS) * jax.nn.sigmoid(ml_o.astype(f32))

    na_out = neighbourhood_attention(na_q.reshape(B, T, NA_HEADS, HEAD_DIM),
                                     na_k.reshape(B, T, NA_HEADS, HEAD_DIM),
                                     na_v.reshape(B, T, NA_HEADS, HEAD_DIM), na_rpb).astype(f32)

    gq = heads(g_q, GLA_HEADS) * (GLA_DK ** -0.5)
    gk = heads(g_k, GLA_HEADS)
    gv = heads(g_v, GLA_HEADS)
    z = jnp.einsum('btzr,zrk->zbtk', g_a.reshape(B, T, 2, GLA_RANK).astype(f32), gla_a_w2.astype(f32))
    z = z + gla_a_b.astype(f32)[:, None, None, :]
    log_a = jax.nn.log_sigmoid(z) / GLA_TAU
    log_a = log_a.reshape(2, B, T, GLA_HEADS, GLA_DK).transpose(0, 1, 3, 2, 4)
    o_f = gla_chunked(gq, gk, gv, log_a[0])
    o_b = flip(gla_chunked(flip(gq), flip(gk), flip(gv), flip(log_a[1])))
    gla_h = (o_f + o_b).transpose(0, 2, 1, 3).reshape(B, T, GLA_VDIM)
    gla_out = head_rms_norm(gla_h, gla_norm_g, GLA_HEADS) * jax.nn.silu(g_g.astype(f32))

    mixed = jnp.concatenate([ml_out, na_out, gla_out], axis=-1).astype(h.dtype)
    return mixed @ w_out

def memory_cross_attention(h, mem_n, wq, wk, wv, wo):
    B, T, _ = h.shape
    M = mem_n.shape[1]
    q = (h @ wq).reshape(B, T, X_HEADS, X_HEAD_DIM)
    k = (mem_n @ wk).reshape(B, M, X_HEADS, X_HEAD_DIM)
    v = (mem_n @ wv).reshape(B, M, X_HEADS, X_HEAD_DIM)
    s = jnp.einsum('bthd,bmhd->bhtm', q, k).astype(jnp.float32) * (X_HEAD_DIM ** -0.5)
    p = jax.nn.softmax(s, axis=-1).astype(v.dtype)
    o = jnp.einsum('bhtm,bmhd->bthd', p, v).reshape(B, T, D_MODEL)
    return o @ wo

def conv_ffn(h, w_up, conv_w, conv_b, w_down):
    u = h @ w_up
    a, g = u[..., :D_FF], u[..., D_FF:]
    a = dwconv_centred(a, conv_w, conv_b)
    return (jax.nn.gelu(a) * g) @ w_down

def setup_inputs(seed: int = 0) -> dict:
    key = jax.random.key(seed)
    ks = jax.random.split(key, 26)
    f32 = jnp.float32

    def nrm(k, shape, scale):
        return jax.random.normal(k, shape, f32) * scale

    def gain(k, shape):
        return 1.0 + nrm(k, shape, 0.02)

    f_bias = jnp.linspace(3.0, 6.0, ML_HEADS, dtype=f32)
    zeros_h = jnp.zeros((ML_HEADS,), f32)
    gate_base = jnp.stack([zeros_h, f_bias, zeros_h, f_bias])
    return {
        'x': nrm(ks[0], (BATCH, SEQ, D_MODEL), 1.0),
        'mem': nrm(ks[1], (BATCH, N_MEM, D_MODEL), 1.0),
        'mix_norm_g': gain(ks[2], (DEPTH, D_MODEL)),
        'w_in': nrm(ks[3], (DEPTH, D_MODEL, IN_COLS), D_MODEL ** -0.5),
        'ml_conv_w': nrm(ks[4], (DEPTH, 3, 2 * ML_DIM), 3 ** -0.5),
        'ml_conv_b': nrm(ks[5], (DEPTH, 2 * ML_DIM), 0.02),
        'ml_gate_b': gate_base[None] + nrm(ks[6], (DEPTH, 4, ML_HEADS), 0.1),
        'ml_norm_g': gain(ks[7], (DEPTH, ML_DIM)),
        'na_rpb': nrm(ks[8], (DEPTH, NA_HEADS, 2 * NA_KH_MAX - 1, 2 * NA_KW - 1), 0.1),
        'gla_a_w2': nrm(ks[9], (DEPTH, 2, GLA_RANK, GLA_KDIM), GLA_RANK ** -0.5),
        'gla_a_b': nrm(ks[10], (DEPTH, 2, GLA_KDIM), 0.1),
        'gla_norm_g': gain(ks[11], (DEPTH, GLA_VDIM)),
        'w_out': nrm(ks[12], (DEPTH, D_MIX, D_MODEL), D_MIX ** -0.5),
        'xattn_norm_g': gain(ks[13], (DEPTH, D_MODEL)),
        'mem_norm_g': gain(ks[14], (DEPTH, D_MODEL)),
        'w_xq': nrm(ks[15], (DEPTH, D_MODEL, D_MODEL), D_MODEL ** -0.5),
        'w_xk': nrm(ks[16], (DEPTH, D_MODEL, D_MODEL), D_MODEL ** -0.5),
        'w_xv': nrm(ks[17], (DEPTH, D_MODEL, D_MODEL), D_MODEL ** -0.5),
        'w_xo': nrm(ks[18], (DEPTH, D_MODEL, D_MODEL), D_MODEL ** -0.5),
        'ffn_norm_g': gain(ks[19], (DEPTH, D_MODEL)),
        'w_up': nrm(ks[20], (DEPTH, D_MODEL, 2 * D_FF), D_MODEL ** -0.5),
        'ffn_conv_w': nrm(ks[21], (DEPTH, 3, D_FF), 3 ** -0.5),
        'ffn_conv_b': nrm(ks[22], (DEPTH, D_FF), 0.02),
        'w_down': nrm(ks[23], (DEPTH, D_FF, D_MODEL), D_FF ** -0.5),
        'final_norm_g': gain(ks[24], (D_MODEL,)),
    }

def reference(x, mem, mix_norm_g, w_in, ml_conv_w, ml_conv_b, ml_gate_b, ml_norm_g, na_rpb,
              gla_a_w2, gla_a_b, gla_norm_g, w_out, xattn_norm_g, mem_norm_g,
              w_xq, w_xk, w_xv, w_xo, ffn_norm_g, w_up, ffn_conv_w, ffn_conv_b, w_down,
              final_norm_g):
    h = x
    for l in range(DEPTH):
        h = h + hybrid_mixer(rms_norm(h, mix_norm_g[l]), w_in[l], ml_conv_w[l], ml_conv_b[l],
                             ml_gate_b[l], ml_norm_g[l], na_rpb[l], gla_a_w2[l], gla_a_b[l],
                             gla_norm_g[l], w_out[l])
        h = h + memory_cross_attention(rms_norm(h, xattn_norm_g[l]), rms_norm(mem, mem_norm_g[l]),
                                       w_xq[l], w_xk[l], w_xv[l], w_xo[l])
        h = h + conv_ffn(rms_norm(h, ffn_norm_g[l]), w_up[l], ffn_conv_w[l], ffn_conv_b[l], w_down[l])
    return rms_norm(h, final_norm_g)


_drawn_inputs = setup_inputs


def setup_inputs(seed=0):
    import zlib

    import numpy as np

    out = dict(_drawn_inputs(seed))
    spreads = {}
    factors = {'ml_conv_b': 4.139,
     'ml_norm_g': 5.672,
     'na_rpb': 3.669,
     'gla_norm_g': 5.547,
     'xattn_norm_g': 8.0,
     'mem_norm_g': 8.0,
     'ffn_conv_b': 3.801,
     'final_norm_g': 8.139,
     'ffn_norm_g': 4.177}
    for name, (base, spread) in spreads.items():
        noise = np.random.default_rng([zlib.crc32(name.encode()), seed]).standard_normal(out[name].shape)
        drawn = base * np.exp(spread * noise) if base else spread * noise
        out[name] = __import__('jax').numpy.asarray(drawn.astype(out[name].dtype))
    for name, factor in factors.items():
        out[name] = (out[name] * factor).astype(out[name].dtype)
    return out
```

```python
from contextlib import ExitStack

import concourse.bass as bass
from concourse import mybir

F32 = mybir.dt.float32
F32R = mybir.dt.float32r
ALU = mybir.AluOpType
ACT = mybir.ActivationFunctionType
AX = mybir.AxisListType

P = 128
DM, T, DEPTH = 1024, 256, 2
GW, DH = 64, 64
MLH, NAH, GLH = 6, 5, 5
ML, NA, GK, GV = MLH * DH, NAH * DH, GLH * 32, GLH * DH
TT, KT = T // P, DM // P
RANK, LG = 16, 64
NCH = T // LG
XH, XD = 4, 256
FF = 2816
NP = FF // 256
EPS = 1e-6
NEG = -1e30
C_V, C_O, C_G = 2 * ML, 3 * ML, 4 * ML
C_NQ = C_G + 4 * MLH
C_NK, C_NV = C_NQ + NA, C_NQ + 2 * NA
C_GQ = C_NQ + 3 * NA
C_GK = C_GQ + GK
C_GV = C_GK + GK
C_GG = C_GV + GV
C_GA = C_GG + GV
COLS = C_GA + 2 * RANK

def stream():
    def fm(m, c, n=256):
        return [(m, 0, KT, c, n)]

    def tm(m, c, n):
        return [[(m, k, 4, c, n)] for k in (0, 4)]

    u = [[("w_in", 0, KT, C_G, P), ("w_in", 0, KT, C_NQ, P)], [("w_in", 0, KT, C_NK + 256, P), ("w_in", 0, KT, COLS - P, P)]]
    u += [fm("w_in", 256 * i) for i in range(3)]
    u += [fm("w_in", C_GQ), fm("w_in", C_GK), fm("w_in", C_NQ + P), fm("w_in", C_NK)]
    for c, n in ((C_V, ML), (C_O, ML), (C_NV, NA), (C_GV, GV), (C_GG, GV)):
        u += tm("w_in", c, n)
    u += [fm("w_xk", 256 * i) for i in range(4)]
    u += tm("w_xv", 0, 512) + tm("w_xv", 512, 512)
    u += tm("w_out", 0, 512) + tm("w_out", 512, 512)
    u += [fm("w_xq", 256 * i) for i in range(4)]
    u += tm("w_xo", 0, 512) + tm("w_xo", 512, 512)
    for p in range(NP):
        u += [fm("w_up", 256 * p), fm("w_up", FF + 256 * p)]
        if p:
            u.append([("w_down", 2 * p - 2, 2, 0, DM)])
    u.append([("w_down", 2 * NP - 2, 2, 0, DM)])
    return u

UNITS = stream()
U = len(UNITS)
RING = 3
UW = 2048
assert U % RING == 0
U_XK, U_XV, U_WO, U_XQ, U_XO, U_FF = 19, 23, 27, 31, 35, 39

def unit_a(p):
    return U_FF if p == 0 else U_FF + 2 + 3 * (p - 1)

def unit_d(p):
    return U - 1 if p == NP - 1 else U_FF + 4 + 3 * p

LANDS, SLOT_DMAS = [], [0] * RING
for _u in range(U):
    SLOT_DMAS[_u % RING] += len(UNITS[_u])
    LANDS.append(SLOT_DMAS[_u % RING])

def events():
    j = []

    def job(name, bank, by, unit=None):
        j.append((name, bank, by, unit))

    def tm(unit, names, banks, by):
        j.append((None, None, None, unit))
        job(names[0], banks[0], by)
        job(names[1], banks[1], by, unit + 1)

    job("par", 7, "D")
    for i in range(4):
        job(f"n1_{i}", i, "D")
    for u, (name, b, by) in enumerate((("g_nq", 4, "A"), ("nk_ga", 5, "A"), ("qk0", 6, "D"), ("qk1", 7, "D"), ("qk2", 0, "D"),
                                       ("gq", 1, "A"), ("gk", 2, "A"), ("nq", 3, "A"), ("nk", 4, "A"))):
        job(name, b, by, u)
    for i, (name, b) in enumerate((("v", (5, 6)), ("o", (7, 0)), ("nv", (1, 2)), ("gv", (3, 4)), ("gg", (5, 6)))):
        tm(9 + 2 * i, (name + "0", name + "1"), b, "A")
    for i in range(4):
        job(f"mt_{i}", (7, 0, 1, 2)[i], "D")
    job("gp", 3, "D")
    job("z0", 4, "A")
    job("z1", 5, "A")
    for i in range(4):
        job(f"xk{i}", 6 + i % 2, "A", U_XK + i)
    job("gt", 3, "D")
    for h in range(MLH + 1):
        if h < MLH:
            job(f"mls{h}", h % 2, "D")
            job(f"mlb{h}", 2 + h % 2, "D")
        if h in (1, 3):
            v = h // 2
            tm(U_XV + 2 * v, (f"xv{v}_0", f"xv{v}_1"), (6, 7), "A")
        if h:
            job(f"mlo{h - 1}", 4 + (h - 1) % 2, "A")
    for h in range(NAH + 1):
        if h < NAH:
            job(f"nas{h}", h % 2, "A")
        if h:
            job(f"nat{h - 1}", 2 + (h - 1) % 2, "A")
            job(f"nao{h - 1}", 4 + (h - 1) % 2, "D")
    job("kt0", 6, "D")
    job("kt1", 7, "D")
    for n, b, by in (("ga", 0, "D"), ("kv", 4, "D"), ("go", 0, "A"), ("mx_", 4, "D")):
        for i in range(4):
            job(f"{n}{i}", b + i, by)
    for n in range(2):
        tm(U_WO + 2 * n, (f"wo{n}_0", f"wo{n}_1"), (2 * n, 2 * n + 1), "D")
    for i in range(4):
        job(f"n2_{i}", 4 + i, "D")
    for i in range(4):
        job(f"xq{i}", i, "A", U_XQ + i)
    for n, b, by in (("xs", 4, "A"), ("xt", 0, "A"), ("xo_", 4, "D")):
        for i in range(XH):
            job(f"{n}{i}", b + i, by)
    for n in range(2):
        tm(U_XO + 2 * n, (f"xw{n}_0", f"xw{n}_1"), (2 * n, 2 * n + 1), "D")
    for i in range(4):
        job(f"n3_{i}", 4 + i, "D")
    for p in range(NP + 1):
        if p < NP:
            job(f"fa{p}", 4 + 2 * (p % 2), "D", unit_a(p))
            job(f"fg{p}", 5 + 2 * (p % 2), "D", unit_a(p) + 1)
        if 0 < p < NP:
            j.append((None, None, None, unit_d(p - 1)))
    for i in range(4):
        job(f"fd{i}", i, "D", U - 1 if i == 3 else None)
    return j

EVENTS = events()
NE = len(EVENTS)
JOBS = [(n, b, d) for n, b, d, _ in EVENTS if n]
NJ = len(JOBS)
DONE = {n: i + 1 for i, (n, _, _, _) in enumerate(EVENTS) if n}
USED = {u: i + 1 for i, (_, _, _, u) in enumerate(EVENTS) if u is not None}
assert len(USED) == U
DRAINS = {e: [n for n, _, d in JOBS if d == e] for e in "AD"}
_at = DRAINS["D"].index("mls0")
DRAINS["D"][_at:_at + 2 * MLH] = ["mlb0"] + [f"{k}{h + d}" for h in range(MLH - 1) for k, d in (("mlb", 1), ("mls", 0))] + [f"mls{MLH - 1}"]
DRAIN = {n: (e, i + 1) for e in "AD" for i, n in enumerate(DRAINS[e])}
BANK = {n: b for n, b, _ in JOBS}

def before(name):
    i = [n for n, _, _ in JOBS].index(name)
    for k in range(1, NJ + 1):
        n, b, _ = JOBS[(i - k) % NJ]
        if b == BANK[name]:
            return n, k > i

R_MIX, R_XN, R_MN, R_FN, R_MG = 0, 8, 16, 24, 32
R_CW, R_CB, R_GB = 40, 58, 64
RA = 68
RB_W, RB_B, RB = 0, 66, 88
CHAIN = 512


def build(nc, a, out):
    with ExitStack() as ctx:
        def sb(name, shape, dt=F32):
            return ctx.enter_context(nc.sbuf_tensor(name, shape, dt))

        def sem(name):
            return ctx.enter_context(nc.semaphore(name))

        raw = sb("raw", [P, RING, UW])
        whi = sb("whi", [P, RING, UW], F32R)
        wlo = sb("wlo", [P, RING, UW], F32R)
        h = sb("h", [P, TT, DM])
        tmb = sb("tmb", [P, TT, DM])
        memn = sb("memn", [P, TT, DM])
        xhi = sb("xhi", [P, KT, T], F32R)
        xlo = sb("xlo", [P, KT, T], F32R)
        ss = sb("ss", [P, 12])
        ident = sb("ident", [P, P])
        flip = sb("flip", [P, P])
        ones = sb("ones", [P, T])
        mlm = sb("mlm", [P, 2, T])
        glm = sb("glm", [P, 2, TT, LG])
        bdm = sb("bdm", [P, 4, DH])
        reset = sb("reset", [P, 2 * T])
        win = sb("win", [P, GW])
        perm = sb("perm", [24, 2, 64])
        eps = sb("eps", [P, 1])
        rowa = sb("rowa", [RA, P])
        rowb = sb("rowb", [RB, P])
        pcol = sb("pcol", [P, RA + RB])
        gbias = sb("gbias", [24, 1])
        w2 = sb("w2", [P, 2, 256])
        bt = sb("bt", [P, NAH, 6, GW])
        with ExitStack() as early:
            qk = early.enter_context(nc.sbuf_tensor("qk", [P, 6, T], F32))
            naq = early.enter_context(nc.sbuf_tensor("naq", [P, 3, T], F32))
        fhi = sb("fhi", [P, 2, 2, T], F32R)
        flo = sb("flo", [P, 2, 2, T], F32R)
        sb("early_rest", [P, T])
        nak = sb("nak", [P, 3, T])
        mv = sb("mv", [P, TT, MLH, DH + 1])
        eo = sb("eo", [P, TT, ML])
        nav = sb("nav", [P, TT, NA])
        gv = sb("gv", [P, TT, GV])
        gg = sb("gg", [P, TT, GV])
        eg = sb("eg", [P, TT, GV])
        gq = sb("gq", [P, 2, T])
        gk = sb("gk", [P, 2, T])
        gaT = sb("gaT", [P, T])
        nmax = sb("nmax", [P, 2 * NAH])
        nsum = sb("nsum", [P, 2 * NAH])
        xk = sb("xk", [P, KT, T])
        xv = sb("xv", [P, TT, DM])
        gsb = sb("gsb", [24, T])
        gt = sb("gt", [P, TT, 2, 64])
        em = sb("em", [P, TT, 2, MLH])
        den = sb("den", [P, TT * 2 * MLH])
        den2 = sb("den2", [P, TT * 2 * MLH])
        hs = sb("hs", [P, 32])
        arena = sb("arena", [P, 7936])
        used = [0]

        def carve(*shape, at=None, dt=None):
            n = 1
            for s in shape:
                n *= s
            o = used[0] if at is None else at
            used[0] = o + n
            assert used[0] <= 7936
            v = arena[:, o:o + n]
            if dt:
                v = v.bitcast(dt)
            names = "abcde"[:len(shape)]
            if len(shape) == 1:
                return v
            return v.rearrange(f"p ({' '.join(names)}) -> p {' '.join(names)}", **dict(zip(names[1:], shape[1:])))

        E = carve(2, 768, at=0)
        PT = carve(2, 768)
        qe = carve(6, T)
        gI, gF, gE, gB, gA = (carve(T, at=3072 + i * T)[0:64, :] for i in range(5))
        hraw = carve(TT, 2, MLH, DH + 1, at=4608)
        zs = carve(4, T)
        np_ = carve(2, TT, T, at=0)
        npt = carve(2, TT, TT, P)
        b1 = carve(4, T, at=0)
        b2 = carve(4, T)
        b3 = carve(4, T)
        b4 = carve(4, T)
        ktx = carve(2, TT, P)
        kty = carve(2, TT, 32)
        at = carve(GLH, 2, TT, LG)
        st = carve(2, 3, 320)
        xq = carve(KT, T, at=0)
        xp = carve(XH, TT, T)
        xpt = carve(XH, TT, T)
        fy = carve(2, 2, T, at=0)
        fu = carve(2, 2, T)
        mlh = qk[:, 0:3, :].rearrange("p a b -> p (a b)").rearrange("p (t h d) -> p t h d", t=TT, d=DH)
        sq = qk[:, 3:6, :].rearrange("p a b -> p (a b)").rearrange("p (t h d) -> p t h d", t=TT, d=DH)
        glh = bt[:, 0:2].rearrange("p a b c -> p (a b c)")[:, 0:640].rearrange("p (t h d) -> p t h d", t=TT, d=DH)
        glq = bt[:, 2:4].rearrange("p a b c -> p (a b c)")[:, 0:640].rearrange("p (t h d) -> p t h d", t=TT, d=DH)

        ps = [ctx.enter_context(nc.psum_tensor(f"bank{i}", [P, 512], F32)) for i in range(8)]

        def bank(name, *shape):
            v = ps[BANK[name]][:, :]
            if not shape:
                return v
            names = "abcd"[:len(shape)]
            return v.rearrange(f"p ({' '.join(names)}) -> p {' '.join(names)}", **dict(zip(names[1:], shape[1:])))

        landed = [sem(f"landed{i}") for i in range(RING)]
        hi_done = sem("hi_done")
        lo_done = sem("lo_done")
        te_done = sem("te_done")
        drained = {"A": sem("drained_act"), "D": sem("drained_dve")}
        const_ready = sem("const_ready")
        tok_in = sem("tok_in")
        prm_in = sem("prm_in")
        bt_in = sem("bt_in")
        rstd_ready = sem("rstd_ready")
        xn_ready = sem("xn_ready")
        xhi_ready = sem("xhi_ready")
        mem_rstd = sem("mem_rstd")
        act_pre = sem("act_pre")
        dve_pre = sem("dve_pre")
        pool_chain = sem("pool_chain")
        gfin_in = sem("gfin_in")
        act_chain = sem("act_chain")
        dve_chain = sem("dve_chain")
        conv_ready = sem("conv_ready")
        qkexp_ready = sem("qkexp_ready")
        qk_ready = sem("qk_ready")
        gates_ready = sem("gates_ready")
        gln_ready = sem("gln_ready")
        scan_ready = sem("scan_ready")
        em_ready = sem("em_ready")
        e_ready = sem("e_ready")
        bias_ready = sem("bias_ready")
        nmax_ready = sem("nmax_ready")
        zb_ready = sem("zb_ready")
        zl_ready = sem("zl_ready")
        bc_ready = sem("bc_ready")
        eb_ready = sem("eb_ready")
        qd_ready = sem("qd_ready")
        state_ready = sem("state_ready")
        ln_in = sem("ln_in")
        ln_out = sem("ln_out")
        xmax_ready = sem("xmax_ready")
        xpn_ready = sem("xpn_ready")
        fconv_ready = sem("fconv_ready")
        gelu_ready = sem("gelu_ready")
        fhi_ready = sem("fhi_ready")
        flo_ready = sem("flo_ready")
        fin_ready = sem("fin_ready")
        stored = sem("stored")
        waited = sem("waited")

        prow = [(rowa, R_MIX, 8, P, lambda l: a["mix_norm_g"][bass.ds(l, 1), :].rearrange("o (r c) -> (o r) c", c=P)),
                (rowa, R_XN, 8, P, lambda l: a["xattn_norm_g"][bass.ds(l, 1), :].rearrange("o (r c) -> (o r) c", c=P)),
                (rowa, R_MN, 8, P, lambda l: a["mem_norm_g"][bass.ds(l, 1), :].rearrange("o (r c) -> (o r) c", c=P)),
                (rowa, R_FN, 8, P, lambda l: a["ffn_norm_g"][bass.ds(l, 1), :].rearrange("o (r c) -> (o r) c", c=P)),
                (rowa, R_MG, 3, P, lambda l: a["ml_norm_g"][bass.ds(l, 1), :].rearrange("o (r c) -> (o r) c", c=P)),
                (rowa, R_MG + 6, 2, P, lambda l: a["gla_norm_g"][bass.ds(l, 1), 64:320].rearrange("o (r c) -> (o r) c", c=P)),
                (rowa, R_CW, 18, P, lambda l: a["ml_conv_w"][bass.ds(l, 1)].rearrange("o w (r c) -> (o w r) c", c=P)),
                (rowa, R_CB, 6, P, lambda l: a["ml_conv_b"][bass.ds(l, 1)].rearrange("o (r c) -> (o r) c", c=P)),
                (rowb, RB_W, 66, P, lambda l: a["ffn_conv_w"][bass.ds(l, 1)].rearrange("o w (r c) -> (o w r) c", c=P)),
                (rowb, RB_B, 22, P, lambda l: a["ffn_conv_b"][bass.ds(l, 1)].rearrange("o (r c) -> (o r) c", c=P))]
        NPRM = len(prow) + 1 + 4 + 1 + 2

        def layer_base(pre, per, l, n):
            return l * per + (pre + n)

        def is_filled(eng, l, name):
            eng.wait_ge(te_done, layer_base(NE, NE, l, DONE[name]))

        def is_used(eng, l, u, back=False):
            eng.wait_ge(te_done, layer_base(0 if back else NE, NE, l, USED[u]))

        def slot_left(eng, l, u):
            is_used(eng, l, (u - RING) % U, u < RING)

        def is_drained(eng, l, name, back=False):
            e, i = DRAIN[name]
            n = len(DRAINS[e])
            eng.wait_ge(drained[e], layer_base(0 if back else n, n, l, i))

        def alone(eng):
            eng.sem_inc(waited, 1)

        block = ctx.enter_context(nc.Block())

        @block.sync
        def _(sp):
            for t in range(TT):
                sp.dma_start(h[:, t, :], a["x"][t * P:(t + 1) * P, :]).then_inc(tok_in, 16)
            for t in range(TT):
                sp.dma_start(memn[:, t, :], a["mem"][t * P:(t + 1) * P, :]).then_inc(tok_in, 16)
            with sp.Fori(0, DEPTH) as l:
                row = {m: sp.snap(l * a[m].shape[1]) for m in ("w_in", "w_xk", "w_down")}
                row["w_out"] = row["w_xv"] = row["w_xq"] = row["w_xo"] = row["w_up"] = row["w_xk"]
                row["w_in"] = row["w_xk"]
                lay = sp.snap(l * 1)
                sp.wait_ge(const_ready, 1)
                sp.wait_ge(te_done, layer_base(0, NE, l, DONE["par"]))
                alone(sp)
                for tile, r, n, c, src in prow:
                    sp.dma_start(tile[r:r + n, 0:c], src(lay)).then_inc(prm_in, 16)
                sp.dma_start(rowa[R_MG + 5:R_MG + 6, 64:128], a["gla_norm_g"][bass.ds(lay, 1), 0:64]).then_inc(prm_in, 16)
                for z in range(2):
                    sp.dma_start(rowa[R_GB + 2 * z:R_GB + 2 * z + 1, :],
                                 a["gla_a_b"][bass.ds(lay, 1), z, 0:P]).then_inc(prm_in, 16)
                    sp.dma_start(rowa[R_GB + 2 * z + 1:R_GB + 2 * z + 2, 0:32],
                                 a["gla_a_b"][bass.ds(lay, 1), z, P:GK]).then_inc(prm_in, 16)
                sp.wait_ge(te_done, layer_base(0, NE, l, DONE["z1"]))
                sp.wait_ge(drained["A"], layer_base(0, len(DRAINS["A"]), l, DRAIN["g_nq"][1]))
                alone(sp)
                sp.dma_start(gbias[:, :], a["ml_gate_b"][bass.ds(lay, 1)].rearrange("o g k -> (o g k)").rearrange("(g k) -> g k", k=1)
                             ).then_inc(prm_in, 16)
                for z in range(2):
                    sp.dma_start(w2[96 + RANK * z:96 + RANK * (z + 1), z, 0:GK],
                                 a["gla_a_w2"][bass.ds(lay, 1), z].rearrange("o r k -> (o r) k")).then_inc(prm_in, 16)
                sp.wait_ge(xn_ready, layer_base(0, 4, l, 2))
                alone(sp)
                for half in range(2):
                    for hh in range(NAH):
                        off = (hh * 15 + 5 - half) * 31 - 48
                        v = a["na_rpb"][bass.ds(lay, 1)]
                        src = bass.AP(v.tensor, v.offset + off, [[1, GW], [31, 6], [1, GW]])
                        sp.dma_start(bt[64 * half:64 * half + 64, hh], src).then_inc(bt_in, 16)
                for u in range(U):
                    sp.wait_ge(lo_done, layer_base(0, U, l, u + 1))
                    alone(sp)
                    o = 0
                    for m, k0, nk, c, n in UNITS[u]:
                        dst = raw[:, u % RING, o:o + nk * n].rearrange("p (k n) -> p k n", k=nk)
                        nn = min(n, a[m].shape[2] - c)
                        src = a[m][:, bass.ds(0, a[m].shape[1]), :].rearrange("l r c -> (l r) c")[
                            bass.ds(row[m] + k0 * P, nk * P), c:c + nn].rearrange("(k p) n -> p k n", p=P)
                        sp.dma_start(dst[:, :, 0:nn], src).then_inc(landed[u % RING], 16)
                        o += nk * n
            sp.wait_ge(te_done, NE * DEPTH + DONE["mt_3"])
            g = a["final_norm_g"]
            sp.dma_start(memn[:, 0, :], bass.AP(g.tensor, 0, [[0, P], [1, DM]])).then_inc(gfin_in, 16)
            for t in range(TT):
                sp.wait_ge(fin_ready, t + 1)
                sp.dma_start(out[t * P:(t + 1) * P, :], tmb[:, t, :]).then_inc(stored, 16)
            sp.wait_ge(stored, 16 * TT)

        @block.gpsimd
        def _(pool):
            g = nc.gpsimd
            n = [0]

            def step(ins):
                n[0] += 1
                ins.then_inc(pool_chain, 1)
                pool.wait_ge(pool_chain, n[0])

            def sel(v, op, fill, base, pat, cm):
                step(g.affine_select(out=v, in_=v, compare_op=op, fill=fill, base=base, pattern=pat, channel_multiplier=cm))

            for v, x in ((ident, 0.0), (flip, 0.0), (mlm, 0.0), (glm, 1.0), (bdm, 1.0), (win, 3e38),
                         (perm, 0.0), (ones, 1.0), (reset, 1.0), (rowa, 1.0), (rowb, 1.0), (w2, 0.0), (eps, EPS), (mv, 1.0)):
                step(g.memset(v[:], x))
            for i in range(RING):
                step(g.memset(raw[:, i, :], 0.0))
            sel(ident[:], ALU.not_equal, 1.0, 0, [[-1, P]], 1)
            sel(flip[:].rearrange("p (a c) -> p a c", a=2), ALU.not_equal, 1.0, 63, [[64, 2], [-1, 64]], -1)
            sel(mlm[:, 0, 0:P], ALU.is_ge, NEG, 0, [[1, P]], -1)
            sel(mlm[:, 1, P:T], ALU.is_ge, NEG, 0, [[-1, P]], 1)
            for half in range(2):
                q = slice(64 * half, 64 * half + 64)
                sel(glm[q, 0], ALU.is_ge, 0.0, 0, [[0, TT], [1, LG]], -1)
                sel(glm[q, 1], ALU.is_ge, 0.0, 0, [[0, TT], [-1, LG]], 1)
                sel(win[q, 0:48], ALU.is_ge, NEG, -63 + 8, [[1, 48]], 1)
                sel(win[q, 16:64], ALU.is_ge, NEG, 63 + 7 - 16, [[-1, 48]], -1)
            sel(bdm[:], ALU.is_ge, 0.0, 0, [[-32, 4], [0, DH]], 1)
            sel(bdm[:], ALU.is_ge, 0.0, 31, [[32, 4], [0, DH]], -1)
            for d in range(2):
                for kind in range(2):
                    sel(perm[:, kind, 32 * d:32 * d + MLH], ALU.not_equal, 1.0, -(12 * d + 6 * kind), [[-1, MLH]], 1)
            step(g.memset(reset[:].rearrange("p (c n) -> p c n", n=LG)[:, :, 0:1], 0.0))
            g.memset(hs[:, 31:32], 0.0).then_inc(const_ready, 1)

        @block.tensor
        def _(pe):
            mm = nc.tensor.matmul
            for s, n in ((lo_done, RING), (te_done, NE), (xn_ready, 4),
                         (drained["A"], len(DRAINS["A"])), (drained["D"], len(DRAINS["D"]))):
                pe.sem_inc(s, n)
            pe.wait_ge(const_ready, 1)
            pe.wait_ge(dve_pre, 1)
            with pe.Fori(0, DEPTH) as l:
                def free(name):
                    prev, back = before(name)
                    is_drained(pe, l, prev, back)

                def have(u):
                    pe.wait_ge(lo_done, layer_base(RING, U, l, u + 1))

                def split_mm(o, s_hi, s_lo, m_hi, m_lo, first, last):
                    mm(o, s_hi, m_hi, start=first, stop=False, skip_group_check=True)
                    mm(o, s_hi, m_lo, start=False, stop=False, skip_group_check=True)
                    return mm(o, s_lo, m_hi, start=False, stop=last, skip_group_check=True)

                def fm_unit(u, name):
                    free(name)
                    have(u)
                    o = 0
                    i = 0
                    for m, k0, nk, c, n in UNITS[u]:
                        hi = whi[:, u % RING, o:o + nk * n].rearrange("p (k n) -> p k n", k=nk)
                        lo = wlo[:, u % RING, o:o + nk * n].rearrange("p (k n) -> p k n", k=nk)
                        for f in range(n // P):
                            dst = bank(name, 2, T)[:, i, :]
                            for k in range(KT):
                                cs = slice(f * P, f * P + P)
                                last = split_mm(dst, hi[:, k, cs], lo[:, k, cs], xhi[:, k, :], xlo[:, k, :],
                                                k == 0, k == KT - 1)
                            i += 1
                        o += nk * n
                    last.then_inc(te_done, 1)

                def tm_units(u, names, n):
                    for half in range(2):
                        have(u + half)
                        for t in range(TT):
                            if half == 0:
                                free(names[t])
                            hi = whi[:, (u + half) % RING, 0:4 * n].rearrange("p (k n) -> p k n", k=4)
                            lo = wlo[:, (u + half) % RING, 0:4 * n].rearrange("p (k n) -> p k n", k=4)
                            for k in range(4):
                                kk = 4 * half + k
                                s = slice(t * P, t * P + P)
                                last = split_mm(bank(names[t])[:, 0:n], xhi[:, kk, s], xlo[:, kk, s],
                                                hi[:, k, :], lo[:, k, :], kk == 0, kk == KT - 1)
                            if half or t:
                                last.then_inc(te_done, 1)

                def turn(group, src, i_src):
                    if i_src:
                        pe.wait_ge(xn_ready, layer_base(4, 4, l, i_src))
                    for i in range(4):
                        free(f"{group}_{i}")
                        o = bank(f"{group}_{i}", 2, T)
                        for kk in range(2):
                            k = 2 * i + kk
                            for t in range(TT):
                                last = nc.tensor.transpose(o[:, kk, t * P:(t + 1) * P], src[:, t, k * P:(k + 1) * P], ident[:])
                        last.then_inc(te_done, 1)

                def xt_ready(name):
                    is_drained(pe, l, name)

                pe.wait_ge(prm_in, layer_base(0, 16 * NPRM, l, 16 * NPRM))
                free("par")
                nc.tensor.transpose(bank("par")[:, 0:RA], rowa[:, :], ident[0:RA, 0:RA])
                nc.tensor.transpose(bank("par")[:, P:P + RB], rowb[:, :], ident[0:RB, 0:RB]).then_inc(te_done, 1)
                turn("n1", tmb, 1)
                xt_ready("n1_3")
                for u, name in enumerate(("g_nq", "nk_ga", "qk0", "qk1", "qk2", "gq", "gk", "nq", "nk")):
                    fm_unit(u, name)
                for i, (nm, n) in enumerate((("v", ML), ("o", ML), ("nv", NA), ("gv", GV), ("gg", GV))):
                    tm_units(9 + 2 * i, (nm + "0", nm + "1"), n)
                turn("mt", memn, 0)
                free("gp")
                is_drained(pe, l, "g_nq")
                mm(bank("gp")[0:64, 0:T], perm[:, 0, :], gsb[:, :], start=True, stop=True)
                mm(bank("gp")[0:64, T:2 * T], perm[:, 1, :], gsb[:, :], start=True, stop=True).then_inc(te_done, 1)
                is_drained(pe, l, "nk_ga")
                for z in range(2):
                    free(f"z{z}")
                    for d in range(2):
                        last = mm(bank(f"z{z}", 2, T)[:, d, :], w2[96:128, d, P * z:P * z + P], gaT[96:128, :], start=True, stop=True)
                    last.then_inc(te_done, 1)
                xt_ready("mt_3")
                for i in range(4):
                    fm_unit(U_XK + i, f"xk{i}")
                free("gt")
                pe.wait_ge(scan_ready, layer_base(0, 1, l, 1))
                alone(pe)
                for t in range(TT):
                    nc.tensor.transpose(bank("gt", 4, P)[:, 2 * t, 0:64], gI[:, t * P:(t + 1) * P], ident[0:64, 0:64])
                    last = nc.tensor.transpose(bank("gt", 4, P)[:, 2 * t + 1, 0:64], gB[:, t * P:(t + 1) * P], ident[0:64, 0:64])
                last.then_inc(te_done, 1)
                pe.wait_ge(qk_ready, layer_base(0, 3, l, 3))
                for hh in range(MLH + 1):
                    if hh < MLH:
                        r, j = slice(64 * (hh % 2), 64 * (hh % 2) + 64), hh // 2
                        free(f"mls{hh}")
                        for jt in range(TT):
                            last = mm(bank(f"mls{hh}", TT, T)[:, jt, :], qk[r, 3 + j, jt * P:(jt + 1) * P], qk[r, j, :], start=True, stop=True)
                        last.then_inc(te_done, 1)
                        free(f"mlb{hh}")
                        for d in range(2):
                            q = 32 * d + hh
                            last = mm(bank(f"mlb{hh}", 2, T)[:, d, :], ident[0:64, q:q + 1].broadcast_to([64, P]), gA[:, :], start=True, stop=True)
                        last.then_inc(te_done, 1)
                    if hh in (1, 3):
                        v = hh // 2
                        tm_units(U_XV + 2 * v, (f"xv{v}_0", f"xv{v}_1"), 512)
                    if hh:
                        g = hh - 1
                        is_drained(pe, l, f"mls{g}")
                        free(f"mlo{g}")
                        w = PT[:, g % 2, :]
                        o = bank(f"mlo{g}")[:, 0:4 * 65].rearrange("p (t d e) -> p t d e", t=TT, d=2)
                        for t, d, src in ((0, 0, ((0, 0),)), (1, 0, ((0, 128), (1, 256))),
                                          (0, 1, ((0, 384), (1, 512))), (1, 1, ((1, 640),))):
                            for i, (jt, c) in enumerate(src):
                                last = mm(o[:, t, d, :], w[:, c:c + P], mv[:, jt, g, :], start=i == 0, stop=i == len(src) - 1)
                        last.then_inc(te_done, 1)
                pe.wait_ge(bias_ready, layer_base(0, 1, l, 1))
                is_drained(pe, l, "nk")
                for hh in range(NAH + 1):
                    if hh < NAH:
                        r, j = slice(64 * (hh % 2), 64 * (hh % 2) + 64), hh // 2
                        free(f"nas{hh}")
                        for t in range(TT):
                            o = bank(f"nas{hh}", TT, T)[:, t, :]
                            b = bt[:, hh, 2 - 2 * t:6 - 2 * t, :].rearrange("p a b -> p (a b)")
                            mm(o, flip[:], b, start=True, stop=False)
                            last = mm(o, naq[r, j, t * P:(t + 1) * P], nak[r, j, :], start=False, stop=True)
                        last.then_inc(te_done, 1)
                    if hh:
                        g = hh - 1
                        is_drained(pe, l, f"nas{g}")
                        free(f"nat{g}")
                        for t in range(TT):
                            for jt in range(TT):
                                last = nc.tensor.transpose(bank(f"nat{g}", TT, TT, P)[:, t, jt, :], np_[:, g % 2, t, jt * P:(jt + 1) * P], ident[:])
                        last.then_inc(te_done, 1)
                        is_drained(pe, l, f"nat{g}")
                        free(f"nao{g}")
                        for t in range(TT):
                            for jt in range(TT):
                                last = mm(bank(f"nao{g}")[:, t * DH:(t + 1) * DH], npt[:, g % 2, t, jt, :],
                                          nav[:, jt, g * DH:(g + 1) * DH], start=jt == 0, stop=jt == 1)
                        last.then_inc(te_done, 1)
                pe.wait_ge(qd_ready, layer_base(0, 1, l, 1))
                free("kt0")
                free("kt1")
                for d in range(2):
                    for t in range(TT):
                        last = nc.tensor.transpose(bank("kt0", 2, TT, P)[:, d, t, :], b4[:, d * 2, t * P:(t + 1) * P], ident[:])
                last.then_inc(te_done, 1)
                for d in range(2):
                    for t in range(TT):
                        last = nc.tensor.transpose(bank("kt1", 4, P)[:, 2 * d + t, 0:32], b4[0:32, d * 2 + 1, t * P:(t + 1) * P], ident[0:32, 0:32])
                last.then_inc(te_done, 1)
                for i in range(4):
                    free(f"ga{i}")
                    for hh in ([0, 4] if i == 0 else [i]):
                        lane, r = (0, slice(32 * hh, 32 * hh + 32)) if hh < 4 else (1, slice(0, 32))
                        for d in range(2):
                            for c in range(NCH):
                                q = slice(64 * (c % 2), 64 * (c % 2) + 64)
                                cc = slice(c * LG, c * LG + LG)
                                last = mm(bank(f"ga{i}", 2, 2, TT, LG)[q, hh // 4, d, c // 2, :], b3[r, 2 * d + lane, cc], b2[r, 2 * d + lane, cc],
                                          start=True, stop=True, skip_group_check=True)
                    last.then_inc(te_done, 1)
                is_drained(pe, l, "kt1")
                for i, lst in enumerate((((0, 0), (0, 2)), ((0, 1), (1, 3)), ((1, 2),), ((1, 1),))):
                    free(f"kv{i}")
                    n = 0
                    for d, c in lst:
                        q = slice(64 * (c % 2), 64 * (c % 2) + 64)
                        last = mm(bank(f"kv{i}", 2, T)[:, n, :], ktx[q, d, c // 2, :], gv[q, c // 2, 0:256], start=True, stop=True, skip_group_check=True)
                        n += 1
                    if i >= 2:
                        for n, (d, c) in enumerate((((0, 0), (0, 2), (1, 2)), ((0, 1), (1, 3), (1, 1)))[i - 2]):
                            q = slice(64 * (c % 2), 64 * (c % 2) + 64)
                            last = mm(bank(f"kv{i}")[0:32, 256 + n * 64:320 + n * 64], kty[q, d, c // 2, :], gv[q, c // 2, 256:320],
                                      start=True, stop=True, skip_group_check=True)
                    last.then_inc(te_done, 1)
                is_drained(pe, l, "ga3")
                pe.wait_ge(state_ready, layer_base(0, 1, l, 1))
                for i in range(4):
                    t, par = i // 2, i % 2
                    c = 2 * t + par
                    q = slice(64 * par, 64 * par + 64)
                    cc = slice(c * LG, c * LG + LG)
                    free(f"go{i}")
                    o = bank(f"go{i}")
                    first = True
                    for d in range(2):
                        n = c if d == 0 else NCH - 1 - c
                        if n:
                            mm(o[q, 0:256], b2[:, 2 * d, cc], st[:, d, n - 1, 0:256], start=first, stop=False, skip_group_check=True)
                            mm(o[q, 256:320], b2[0:32, 2 * d + 1, cc], st[0:32, d, n - 1, 256:320], start=False, stop=False, skip_group_check=True)
                            first = False
                    for d in range(2):
                        for hh in range(GLH):
                            last = mm(o[q, hh * DH:(hh + 1) * DH], at[q, hh, d, t, :], gv[q, t, hh * DH:(hh + 1) * DH],
                                      start=False, stop=d == 1, skip_group_check=True)
                    last.then_inc(te_done, 1)
                turn("mx", tmb, 2)
                xt_ready("mx_3")
                for n in range(2):
                    tm_units(U_WO + 2 * n, (f"wo{n}_0", f"wo{n}_1"), 512)
                turn("n2", tmb, 3)
                xt_ready("n2_3")
                for i in range(4):
                    fm_unit(U_XQ + i, f"xq{i}")
                for hh in range(XH):
                    is_drained(pe, l, f"xq{hh}")
                    free(f"xs{hh}")
                    for t in range(TT):
                        for kk in range(2):
                            last = mm(bank(f"xs{hh}", TT, T)[:, t, :], xq[:, 2 * hh + kk, t * P:(t + 1) * P], xk[:, 2 * hh + kk, :],
                                      start=kk == 0, stop=kk == 1)
                    last.then_inc(te_done, 1)
                for hh in range(XH):
                    pe.wait_ge(xpn_ready, layer_base(0, XH, l, hh + 1))
                    free(f"xt{hh}")
                    for t in range(TT):
                        for jt in range(TT):
                            last = nc.tensor.transpose(bank(f"xt{hh}", TT, T)[:, jt, t * P:(t + 1) * P], xp[:, hh, t, jt * P:(jt + 1) * P], ident[:])
                    last.then_inc(te_done, 1)
                for hh in range(XH):
                    is_drained(pe, l, f"xt{hh}")
                    free(f"xo_{hh}")
                    for f in range(2):
                        for jt in range(TT):
                            last = mm(bank(f"xo_{hh}", 2, T)[:, f, :], xv[:, jt, hh * XD + f * P:hh * XD + (f + 1) * P], xpt[:, hh, jt, :],
                                      start=jt == 0, stop=jt == 1)
                    last.then_inc(te_done, 1)
                xt_ready("xo_3")
                for n in range(2):
                    tm_units(U_XO + 2 * n, (f"xw{n}_0", f"xw{n}_1"), 512)
                turn("n3", tmb, 4)
                xt_ready("n3_3")
                for p in range(NP + 1):
                    if p < NP:
                        fm_unit(unit_a(p), f"fa{p}")
                        fm_unit(unit_a(p) + 1, f"fg{p}")
                    if p:
                        g = p - 1
                        u = unit_d(g)
                        have(u)
                        pe.wait_ge(flo_ready, layer_base(0, NP, l, g + 1))
                        hi = whi[:, u % RING, :].rearrange("p (k n) -> p k n", k=2)
                        lo = wlo[:, u % RING, :].rearrange("p (k n) -> p k n", k=2)
                        for n in range(2):
                            for t in range(TT):
                                if g == 0:
                                    free(f"fd{2 * n + t}")
                                for k in range(2):
                                    s = slice(t * P, t * P + P)
                                    last = split_mm(bank(f"fd{2 * n + t}"), fhi[:, g % 2, k, s], flo[:, g % 2, k, s],
                                                    hi[:, k, n * 512:(n + 1) * 512], lo[:, k, n * 512:(n + 1) * 512],
                                                    g == 0 and k == 0, g == NP - 1 and k == 1)
                                if g == NP - 1 or (n, t) == (1, 1):
                                    last.then_inc(te_done, 1)

        @block.scalar
        def _(act):
            A = nc.scalar.activation
            n_chain = [0]

            def rms(src, junk, s, link, width=DM):
                for t in range(TT):
                    ins = A(junk[:, t, :], src[:, t, :], ACT.Square, accum_out=ss[:, s + t:s + t + 1])
                link(ins)
                link(A(ss[:, s:s + 2], ss[:, s:s + 2], ACT.Ln, scale=1.0 / width, bias=eps[:, :]))
                return A(ss[:, s:s + 2], ss[:, s:s + 2], ACT.Exp, scale=-0.5)

            def pre_link(ins):
                n_chain[0] += 1
                ins.then_inc(act_pre, 1)
                act.wait_ge(act_pre, n_chain[0])

            act.wait_ge(const_ready, 1)
            act.wait_ge(tok_in, 16 * 2 * TT)
            rms(memn, tmb, 0, pre_link).then_inc(mem_rstd, 1)
            with act.Fori(0, DEPTH) as l:
                chain = [0]

                def link(ins):
                    chain[0] += 1
                    ins.then_inc(act_chain, 1)
                    act.wait_ge(act_chain, layer_base(0, CHAIN, l, chain[0]))

                nhi = [0]

                def split_hi(upto):
                    while nhi[0] < min(upto, U):
                        u = nhi[0]
                        act.wait_ge(landed[u % RING], layer_base(0, 16 * SLOT_DMAS[u % RING], l, 16 * LANDS[u]))
                        slot_left(act, l, u)
                        n = sum(x[2] * x[4] for x in UNITS[u])
                        A(whi[:, u % RING, 0:n], raw[:, u % RING, 0:n], ACT.Copy).then_inc(hi_done, 1)
                        nhi[0] += 1

                def norm(job, s, back=False):
                    is_drained(act, l, job, back)
                    rms(h, tmb, s, link).then_inc(rstd_ready, 1)

                def turned(group, gcol, n=4):
                    for i in range(n):
                        is_filled(act, l, f"{group}_{i}")
                        for kk in range(2):
                            k = 2 * i + kk
                            last = A(xhi[:, k, :], bank(f"{group}_{i}", 2, T)[:, kk, :], ACT.Copy, scale=pcol[:, gcol + k:gcol + k + 1])
                        last.then_inc(xhi_ready, 1)

                def drain(ins):
                    ins.then_inc(drained["A"], 1)

                norm("fd3", 2, True)
                split_hi(3)
                is_drained(act, l, "par")
                turned("n1", R_MIX)
                is_filled(act, l, "g_nq")
                split_hi(3)
                A(gsb[:, :], bank("g_nq", 2, T)[0:24, 0, :], ACT.Identity, bias=gbias[:, :])
                drain(A(naq[:, 0, :], bank("g_nq", 2, T)[:, 1, :], ACT.Copy, scale=DH ** -0.5))
                split_hi(4)
                is_filled(act, l, "nk_ga")
                A(nak[:, 2, :], bank("nk_ga", 2, T)[:, 0, :], ACT.Copy)
                drain(A(gaT[96:128, :], bank("nk_ga", 2, T)[96:128, 1, :], ACT.Copy))
                for i in range(3):
                    split_hi(5 + i)
                    is_filled(act, l, f"qk{i}")
                    for f in range(2):
                        j = 2 * i + f
                        last = A(qk[:, j, :], bank(f"qk{i}", 2, T)[:, f, :], ACT.Identity,
                                 scale=pcol[:, R_CW + 6 + j:R_CW + 7 + j], bias=pcol[:, R_CB + j:R_CB + j + 1])
                    last.then_inc(conv_ready, 1)
                split_hi(8)
                is_filled(act, l, "gq")
                drain(A(gq[:], bank("gq", 2, T), ACT.Copy, scale=32 ** -0.5))
                for i in range(3):
                    is_drained(act, l, f"qk{i}")
                    A(qe[:, 2 * i:2 * i + 2, :], qk[:, 2 * i:2 * i + 2, :], ACT.Exp, scale=-1.0).then_inc(qkexp_ready, 1)
                split_hi(9)
                is_filled(act, l, "gk")
                drain(A(gk[:], bank("gk", 2, T), ACT.Copy))
                split_hi(10)
                is_filled(act, l, "nq")
                drain(A(naq[:, 1:3, :], bank("nq", 2, T), ACT.Copy, scale=DH ** -0.5))
                split_hi(11)
                is_filled(act, l, "nk")
                drain(A(nak[:, 0:2, :], bank("nk", 2, T), ACT.Copy))
                for i, nm in enumerate(("v", "o", "nv", "gv", "gg")):
                    for t in range(TT):
                        split_hi(12 + 2 * i + t)
                        is_filled(act, l, f"{nm}{t}")
                        b = bank(f"{nm}{t}")
                        if nm == "v":
                            drain(A(mv[:, t, :, 0:DH], b[:, 0:ML].rearrange("p (h d) -> p h d", d=DH), ACT.Copy))
                        elif nm == "o":
                            drain(A(eo[:, t, :], b[:, 0:ML], ACT.Exp, scale=-1.0))
                        elif nm == "gg":
                            A(gg[:, t, :], b[:, 0:GV], ACT.Copy)
                            drain(A(eg[:, t, :], b[:, 0:GV], ACT.Exp, scale=-1.0))
                        else:
                            drain(A((nav if nm == "nv" else gv)[:, t, :], b[:, 0:GV], ACT.Copy))
                split_hi(22)
                turned("mt", R_MN)
                act.wait_ge(gates_ready, layer_base(0, 1, l, 1))
                link(A(gE[:, :], gE[:, :], ACT.Exp))
                A(gE[:, :], gE[:, :], ACT.Ln, bias=ones[0:64, 0:1]).then_inc(gln_ready, 1)
                for z in range(2):
                    is_filled(act, l, f"z{z}")
                    for d in range(2):
                        last = A(zs[:, 2 * d + z, :], bank(f"z{z}", 2, T)[:, d, :], ACT.Identity,
                                 bias=pcol[:, R_GB + 2 * d + z:R_GB + 2 * d + z + 1])
                    drain(last)
                for i in range(4):
                    split_hi(U_XK + i + 3)
                    is_filled(act, l, f"xk{i}")
                    drain(A(xk[:, 2 * i:2 * i + 2, :], bank(f"xk{i}", 2, T), ACT.Copy))
                is_drained(act, l, "gt")
                for d in range(2):
                    last = A(em[:, :, d, :], gt[:, :, 1, 32 * d:32 * d + MLH], ACT.Exp, scale=-1.0)
                last.then_inc(em_ready, 1)
                for hh in range(MLH + 1):
                    if hh < MLH:
                        is_drained(act, l, f"mlb{hh}")
                        A(E[:, hh % 2, :], E[:, hh % 2, :], ACT.Exp).then_inc(e_ready, 1)
                    if hh in (1, 3):
                        v = hh // 2
                        for t in range(TT):
                            split_hi(U_XV + 2 * v + 3)
                            is_filled(act, l, f"xv{v}_{t}")
                            drain(A(xv[:, t, 512 * v:512 * v + 512], bank(f"xv{v}_{t}"), ACT.Copy))
                    if hh:
                        g = hh - 1
                        is_filled(act, l, f"mlo{g}")
                        drain(A(hraw[:, :, :, g, :], bank(f"mlo{g}")[:, 0:260].rearrange("p (t d e) -> p t d e", t=TT, d=2), ACT.Copy))
                split_hi(U_XV + 4 + 3)
                for hh in range(NAH + 1):
                    if hh < NAH:
                        act.wait_ge(nmax_ready, layer_base(0, NAH, l, hh + 1))
                        for t in range(TT):
                            last = A(np_[:, hh % 2, t, :], bank(f"nas{hh}", TT, T)[:, t, :], ACT.Exp,
                                     bias=nmax[:, 2 * hh + t:2 * hh + t + 1], accum_out=nsum[:, 2 * hh + t:2 * hh + t + 1])
                        drain(last)
                    if hh:
                        is_filled(act, l, f"nat{hh - 1}")
                        drain(A(npt[:, (hh - 1) % 2].rearrange("p a b c -> p (a b c)"), bank(f"nat{hh - 1}"), ACT.Copy))
                act.wait_ge(zb_ready, layer_base(0, 1, l, 1))
                link(A(b2[:], b2[:], ACT.Exp))
                A(b2[:], b2[:], ACT.Ln, bias=ones[:, 0:1]).then_inc(zl_ready, 1)
                act.wait_ge(bc_ready, layer_base(0, 1, l, 1))
                A(b1[:], b2[:], ACT.Exp, scale=1.0 / 16).then_inc(eb_ready, 1)
                A(b3[:], b2[:], ACT.Exp, scale=-1.0 / 16).then_inc(eb_ready, 1)
                def head_scale(v, n, i):
                    act.wait_ge(ln_in, layer_base(0, 2, l, i))
                    link(A(v, v, ACT.Ln, scale=1.0 / DH, bias=eps[:, :]))
                    A(v, v, ACT.Exp, scale=-0.5).then_inc(ln_out, 1)

                head_scale(hs[:, 0:12], 12, 1)
                for i in range(4):
                    is_filled(act, l, f"go{i}")
                    q = slice(64 * (i % 2), 64 * (i % 2) + 64)
                    drain(A(glh[q, i // 2].rearrange("p h d -> p (h d)"), bank(f"go{i}")[q, 0:GV], ACT.Copy))
                head_scale(hs[:, 12:22], 10, 2)
                split_hi(U_WO + 3)
                turned("mx", R_MG)
                split_hi(U_WO + 4 + 2)
                norm("wo1_1", 4)
                split_hi(U_XQ + 3)
                turned("n2", R_XN)
                for i in range(4):
                    split_hi(U_XQ + i + 3)
                    is_filled(act, l, f"xq{i}")
                    drain(A(xq[:, 2 * i:2 * i + 2, :], bank(f"xq{i}", 2, T), ACT.Copy, scale=XD ** -0.5))
                for hh in range(XH):
                    act.wait_ge(xmax_ready, layer_base(0, XH, l, hh + 1))
                    for t in range(TT):
                        last = A(xp[:, hh, t, :], bank(f"xs{hh}", TT, T)[:, t, :], ACT.Exp,
                                 bias=nmax[:, 2 * hh + t:2 * hh + t + 1], accum_out=nsum[:, 2 * hh + t:2 * hh + t + 1])
                    drain(last)
                for hh in range(XH):
                    is_filled(act, l, f"xt{hh}")
                    drain(A(xpt[:, hh].rearrange("p a b -> p (a b)"), bank(f"xt{hh}"), ACT.Copy))
                for hh in range(XH):
                    is_filled(act, l, f"xo_{hh}")
                    A(xhi[:, 2 * hh:2 * hh + 2, :], bank(f"xo_{hh}", 2, T), ACT.Copy).then_inc(xhi_ready, 1)
                split_hi(U_XO + 4 + 2)
                norm("xw1_1", 6)
                split_hi(U_FF + 3)
                turned("n3", R_FN)
                for p in range(NP):
                    split_hi(unit_a(p) + 3)
                    is_filled(act, l, f"fa{p}")
                    for f in range(2):
                        j = 2 * p + f
                        last = A(fy[:, p % 2, f, :], bank(f"fa{p}", 2, T)[:, f, :], ACT.Identity,
                                 scale=pcol[:, RA + RB_W + 22 + j:RA + RB_W + 23 + j], bias=pcol[:, RA + RB_B + j:RA + RB_B + j + 1])
                    last.then_inc(fconv_ready, 1)
                    split_hi(unit_a(p) + 4)
                    is_drained(act, l, f"fa{p}")
                    A(fy[:, p % 2], fy[:, p % 2], ACT.Gelu_apprx_tanh).then_inc(gelu_ready, 1)
                    is_drained(act, l, f"fg{p}")
                    A(fhi[:, p % 2], fu[:, p % 2], ACT.Copy).then_inc(fhi_ready, 1)
                split_hi(U)
                act.sem_inc(act_chain, CHAIN - chain[0])
            act.wait_ge(drained["D"], len(DRAINS["D"]) * (DEPTH + 1))
            rms(h, tmb, 8, pre_link).then_inc(mem_rstd, 1)

        @block.vector
        def _(dve):
            V = nc.vector
            ts, tt, stt = V.tensor_scalar, V.tensor_tensor, V.scalar_tensor_tensor
            dve.wait_ge(const_ready, 1)
            dve.wait_ge(tok_in, 16 * 2 * TT)
            dve.wait_ge(mem_rstd, 1)
            for t in range(TT):
                last = ts(memn[:, t, :], memn[:, t, :], ss[:, t:t + 1], None, ALU.mult)
            last.then_inc(dve_pre, 1)
            dve.wait_ge(dve_pre, 1)
            with dve.Fori(0, DEPTH) as l:
                chain = [0]

                def link(ins):
                    chain[0] += 1
                    ins.then_inc(dve_chain, 1)
                    dve.wait_ge(dve_chain, layer_base(0, CHAIN, l, chain[0]))

                nlo = [0]

                def split_lo(upto):
                    while nlo[0] < min(upto, U):
                        u = nlo[0]
                        dve.wait_ge(hi_done, layer_base(0, U, l, u + 1))
                        n = sum(x[2] * x[4] for x in UNITS[u])
                        tt(wlo[:, u % RING, 0:n], raw[:, u % RING, 0:n], whi[:, u % RING, 0:n], ALU.subtract).then_inc(lo_done, 1)
                        nlo[0] += 1

                def drain(ins):
                    ins.then_inc(drained["D"], 1)

                def normed(i, s):
                    dve.wait_ge(rstd_ready, layer_base(0, 3, l, i + 1))
                    for t in range(TT):
                        last = ts(tmb[:, t, :], h[:, t, :], ss[:, s + t:s + t + 1], None, ALU.mult)
                    last.then_inc(xn_ready, 1)

                xh = [0]

                def turned(group, gcol):
                    for i in range(4):
                        xh[0] += 1
                        dve.wait_ge(xhi_ready, layer_base(0, 24, l, xh[0]))
                        for kk in range(2):
                            k = 2 * i + kk
                            last = stt(xlo[:, k, :], bank(f"{group}_{i}", 2, T)[:, kk, :], pcol[:, gcol + k:gcol + k + 1], xhi[:, k, :],
                                       ALU.mult, ALU.subtract)
                        drain(last)

                def residual(name, u):
                    for n in range(2):
                        for t in range(TT):
                            split_lo(u + 2 * n + t + 3)
                            is_filled(dve, l, f"{name}{n}_{t}")
                            hh = h[:, t, n * 512:(n + 1) * 512]
                            last = tt(hh, hh, bank(f"{name}{n}_{t}"), ALU.add)
                            drain(last)
                    is_drained(dve, l, f"{name}1_1")

                normed(0, 2)
                is_filled(dve, l, "par")
                V.tensor_copy(pcol[:, 0:RA], bank("par")[:, 0:RA])
                drain(V.tensor_copy(pcol[:, RA:RA + RB], bank("par")[:, P:P + RB]))
                split_lo(3)
                turned("n1", R_MIX)
                dve.wait_ge(bt_in, layer_base(0, 16 * 2 * NAH, l, 16 * 2 * NAH))
                bv = bt[:].rearrange("p a b c -> p (a b) c")
                tt(bv, bv, win[:].rearrange("p (o c) -> p o c", o=1).broadcast_to([P, 6 * NAH, GW]), ALU.min).then_inc(bias_ready, 1)
                split_lo(4)
                for i in range(3):
                    split_lo(5 + i)
                    dve.wait_ge(conv_ready, layer_base(0, 3, l, i + 1))
                    y = qk[:, 2 * i:2 * i + 2, :]
                    b = bank(f"qk{i}", 2, T)
                    for f in range(2):
                        j = 2 * i + f
                        ins = stt(y[:, f, 1:T], b[:, f, 0:T - 1], pcol[:, R_CW + j:R_CW + j + 1], y[:, f, 1:T], ALU.mult, ALU.add)
                    link(ins)
                    for f in range(2):
                        j = 2 * i + f
                        ins = stt(y[:, f, 0:T - 1], b[:, f, 1:T], pcol[:, R_CW + 12 + j:R_CW + 13 + j], y[:, f, 0:T - 1], ALU.mult, ALU.add)
                    drain(ins)
                split_lo(9)
                for i in range(3):
                    dve.wait_ge(qkexp_ready, layer_base(0, 3, l, i + 1))
                    e = qe[:, 2 * i:2 * i + 2, :]
                    link(ts(e, e, 1.0, None, ALU.add))
                    link(V.reciprocal(e, e))
                    tt(qk[:, 2 * i:2 * i + 2, :], qk[:, 2 * i:2 * i + 2, :], e, ALU.mult).then_inc(qk_ready, 1)
                split_lo(22)
                turned("mt", R_MN)
                is_filled(dve, l, "gp")
                V.tensor_copy(gI[:, :], bank("gp")[0:64, 0:T])
                drain(V.tensor_copy(gF[:, :], bank("gp")[0:64, T:2 * T]))
                is_drained(dve, l, "gp")
                stt(gE[:, :], gF[:, :], -1.0, gF[:, :], ALU.mult, ALU.min).then_inc(gates_ready, 1)
                dve.wait_ge(gln_ready, layer_base(0, 1, l, 1))
                link(stt(gF[:, :], gF[:, :], 0.0, gE[:, :], ALU.min, ALU.subtract))
                V.tensor_tensor_scan(gB[0:32, :], ones[0:32, :], gF[0:32, :], 0.0, ALU.mult, ALU.add)
                link(V.tensor_tensor_scan(gB[32:64, ::-1], ones[32:64, :], gF[32:64, ::-1], 0.0, ALU.mult, ALU.add))
                link(tt(gI[:, :], gI[:, :], gB[:, :], ALU.subtract))
                V.tensor_tensor_scan(gA[0:32, :], gI[0:32, :], gI[0:32, :], 0.0, ALU.max, ALU.max)
                link(V.tensor_tensor_scan(gA[32:64, ::-1], gI[32:64, ::-1], gI[32:64, ::-1], 0.0, ALU.max, ALU.max))
                link(tt(gB[:, :], gB[:, :], gA[:, :], ALU.add))
                ts(gA[:, :], gA[:, :], -1.0, None, ALU.mult).then_inc(scan_ready, 1)
                for i in range(4):
                    split_lo(U_XK + i + 3)
                is_filled(dve, l, "gt")
                V.tensor_copy(gt[:].rearrange("p t k c -> p (t k) c"), bank("gt", 4, P)[:, :, 0:64]).then_inc(drained["D"], 1)
                is_drained(dve, l, "gt")
                for hh in range(MLH + 1):
                    if hh < MLH:
                        is_filled(dve, l, f"mlb{hh}")
                        nb = bank(f"mlb{hh}", 2, T)
                        e = E[:, hh % 2, :]

                        def aj(t, d):
                            return gt[:, t, 0, 32 * d + hh:32 * d + hh + 1]

                        stt(e[:, 0:256], nb[:, 0, :], aj(0, 0), mlm[:, 0, :], ALU.add, ALU.min)
                        stt(e[:, 256:384], nb[:, 0, P:T], aj(1, 0), mlm[:, 0, 0:P], ALU.add, ALU.min)
                        stt(e[:, 384:512], nb[:, 1, 0:P], aj(0, 1), mlm[:, 1, P:T], ALU.add, ALU.min)
                        drain(stt(e[:, 512:768], nb[:, 1, :], aj(1, 1), mlm[:, 1, :], ALU.add, ALU.min))
                    if hh in (1, 3):
                        split_lo(U_XV + 2 * (hh // 2) + 3)
                    if hh:
                        g = hh - 1
                        dve.wait_ge(e_ready, layer_base(0, MLH, l, g + 1))
                        if g >= 2:
                            is_filled(dve, l, f"mlo{g - 2}")
                        s = bank(f"mls{g}", TT, T)
                        e, w = E[:, g % 2, :], PT[:, g % 2, :]
                        sc = DH ** -0.5
                        stt(w[:, 0:256], s[:, 0, :], sc, e[:, 0:256], ALU.mult, ALU.mult)
                        stt(w[:, 256:384], s[:, 1, P:T], sc, e[:, 256:384], ALU.mult, ALU.mult)
                        stt(w[:, 384:512], s[:, 0, 0:P], sc, e[:, 384:512], ALU.mult, ALU.mult)
                        drain(stt(w[:, 512:768], s[:, 1, :], sc, e[:, 512:768], ALU.mult, ALU.mult))
                split_lo(U_XV + 4 + 3)
                is_drained(dve, l, f"mlo{MLH - 1}")
                dve.wait_ge(em_ready, layer_base(0, 1, l, 1))
                hr = hraw[:].rearrange("p t d h e -> p (t d h) e")
                link(stt(den[:, :], hr[:, :, DH], -1.0, hr[:, :, DH], ALU.mult, ALU.max))
                link(tt(den[:, :], den[:, :], em[:].rearrange("p t d h -> p (t d h)"), ALU.max))
                link(V.reciprocal(den[:, :], den[:, :]))
                link(tt(hr[:, :, 0:DH], hr[:, :, 0:DH], den[:].rearrange("p (n o) -> p n o", o=1).broadcast_to([P, 24, DH]), ALU.mult))
                link(tt(mlh, hraw[:, :, 0, :, 0:DH], hraw[:, :, 1, :, 0:DH], ALU.add))
                link(ts(eo[:], eo[:], 1.0, None, ALU.add))
                link(V.reciprocal(eo[:], eo[:]))
                link(tt(sq, mlh, mlh, ALU.mult))
                V.reduce_sum(hs[:, 0:12].rearrange("p (t h) -> p t h", t=TT), sq, AX.X).then_inc(ln_in, 1)
                for hh in range(NAH + 1):
                    if hh < NAH:
                        is_filled(dve, l, f"nas{hh}")
                        link(V.tensor_reduce(nmax[:, 2 * hh:2 * hh + 2], bank(f"nas{hh}", TT, T), AX.X, ALU.max))
                        ts(nmax[:, 2 * hh:2 * hh + 2], nmax[:, 2 * hh:2 * hh + 2], -1.0, None, ALU.mult).then_inc(nmax_ready, 1)
                    if hh:
                        g = hh - 1
                        is_drained(dve, l, f"nas{g}")
                        link(V.reciprocal(nsum[:, 2 * g:2 * g + 2], nsum[:, 2 * g:2 * g + 2]))
                        is_filled(dve, l, f"nao{g}")
                        for t in range(TT):
                            last = ts(tmb[:, t, ML + g * DH:ML + (g + 1) * DH], bank(f"nao{g}")[:, t * DH:(t + 1) * DH],
                                      nsum[:, 2 * g + t:2 * g + t + 1], None, ALU.mult)
                        drain(last)
                is_drained(dve, l, "z1")
                stt(b2[:], zs[:], -1.0, zs[:], ALU.mult, ALU.min).then_inc(zb_ready, 1)
                dve.wait_ge(zl_ready, layer_base(0, 1, l, 1))
                link(stt(b1[:], zs[:], 0.0, b2[:], ALU.min, ALU.subtract))
                la = b1[:].rearrange("p a b -> p (a b)")
                bc = b2[:].rearrange("p a b -> p (a b)")
                V.tensor_tensor_scan(bc[:, 0:512], reset[:], la[:, 0:512], 0.0, ALU.mult, ALU.add)
                V.tensor_tensor_scan(bc[:, 1023:511:-1], reset[:], la[:, 1023:511:-1], 0.0, ALU.mult, ALU.add).then_inc(bc_ready, 1)
                dve.wait_ge(eb_ready, layer_base(0, 2, l, 2))
                for d in range(2):
                    tt(b2[:, 2 * d:2 * d + 2, :], gq[:], b1[:, 2 * d:2 * d + 2, :], ALU.mult)
                    ins = tt(b3[:, 2 * d:2 * d + 2, :], gk[:], b3[:, 2 * d:2 * d + 2, :], ALU.mult)
                link(ins)
                for d in range(2):
                    cv = lambda v: v[:, 2 * d:2 * d + 2, :].rearrange("p a (c n) -> p (a c) n", n=LG)
                    e = cv(b1)[:, :, (LG - 1) * (1 - d):(LG - 1) * (1 - d) + 1]
                    last = tt(cv(b4), cv(b3), e.broadcast_to([P, 2 * NCH, LG]), ALU.mult)
                last.then_inc(qd_ready, 1)
                is_filled(dve, l, "kt0")
                drain(V.tensor_copy(ktx[:].rearrange("p a b c -> p (a b c)"), bank("kt0")))
                is_filled(dve, l, "kt1")
                drain(V.tensor_copy(kty[:].rearrange("p a b c -> p (a b) c"), bank("kt1", 4, P)[:, :, 0:32]))
                for i in range(4):
                    is_filled(dve, l, f"ga{i}")
                    for hh in ([4, 0] if i == 0 else [i]):
                        last = tt(at[:, hh].rearrange("p a b c -> p (a b c)"), bank(f"ga{i}", 2, T)[:, hh // 4, :],
                                  glm[:].rearrange("p a b c -> p (a b c)"), ALU.mult)
                    drain(last)
                for i in range(4):
                    is_filled(dve, l, f"kv{i}")
                bd = bdm[:].rearrange("p a b -> p (a b)")
                where = {(0, 0): ("kv0", 0, "kv2", 0), (0, 2): ("kv0", 1, "kv2", 1), (0, 1): ("kv1", 0, "kv3", 0),
                         (1, 3): ("kv1", 1, "kv3", 1), (1, 2): ("kv2", 0, "kv2", 2), (1, 1): ("kv3", 0, "kv3", 2)}
                for d in range(2):
                    for n in range(3):
                        c = n if d == 0 else NCH - 1 - n
                        jx, ix, jy, iy = where[d, c]
                        tt(st[:, d, n, 0:256], bank(jx, 2, T)[:, ix, :], bd, ALU.mult)
                        ins = V.tensor_copy(st[0:32, d, n, 256:320], bank(jy)[0:32, 256 + 64 * iy:320 + 64 * iy])
                link(ins)
                dve.sem_inc(drained["D"], 4)
                for n in range(1, 3):
                    for d in range(2):
                        c = n if d == 0 else NCH - 1 - n
                        e = c * LG + (LG - 1) * (1 - d)
                        stt(st[:, d, n, 0:256], st[:, d, n - 1, 0:256], b1[:, 2 * d, e:e + 1], st[:, d, n, 0:256], ALU.mult, ALU.add)
                        ins = stt(st[0:32, d, n, 256:320], st[0:32, d, n - 1, 256:320], b1[0:32, 2 * d + 1, e:e + 1],
                                  st[0:32, d, n, 256:320], ALU.mult, ALU.add)
                    if n == 1:
                        link(ins)
                ins.then_inc(state_ready, 1)

                def scaled(v, n, c, width, gate, i):
                    dve.wait_ge(ln_out, layer_base(0, 2, l, i))
                    nh = width // DH
                    s = hs[:, n:n + 2 * nh].rearrange("p (t h o) -> p t h o", t=TT, o=1)
                    for t in range(TT):
                        ins = tt(v[:, t], v[:, t], s[:, t].broadcast_to([P, nh, DH]), ALU.mult)
                    link(ins)
                    return tt(tmb[:, :, c:c + width], v.rearrange("p t h d -> p t (h d)"), gate[:], ALU.mult)

                scaled(mlh, 0, 0, ML, eo, 1)
                link(ts(eg[:], eg[:], 1.0, None, ALU.add))
                link(V.reciprocal(eg[:], eg[:]))
                link(tt(gg[:], gg[:], eg[:], ALU.mult))
                is_drained(dve, l, "go3")
                link(tt(glq, glh, glh, ALU.mult))
                V.reduce_sum(hs[:, 12:22].rearrange("p (t h) -> p t h", t=TT), glq, AX.X).then_inc(ln_in, 1)
                scaled(glh, 12, ML + NA, GV, gg, 2).then_inc(xn_ready, 1)
                split_lo(U_WO + 3)
                turned("mx", R_MG)
                residual("wo", U_WO)
                normed(1, 4)
                split_lo(U_XQ + 3)
                turned("n2", R_XN)
                for i in range(4):
                    split_lo(U_XQ + i + 3)
                for hh in range(XH):
                    is_filled(dve, l, f"xs{hh}")
                    link(V.tensor_reduce(nmax[:, 2 * hh:2 * hh + 2], bank(f"xs{hh}", TT, T), AX.X, ALU.max))
                    ts(nmax[:, 2 * hh:2 * hh + 2], nmax[:, 2 * hh:2 * hh + 2], -1.0, None, ALU.mult).then_inc(xmax_ready, 1)
                for hh in range(XH):
                    is_drained(dve, l, f"xs{hh}")
                    link(V.reciprocal(nsum[:, 2 * hh:2 * hh + 2], nsum[:, 2 * hh:2 * hh + 2]))
                    for t in range(TT):
                        last = ts(xp[:, hh, t, :], xp[:, hh, t, :], nsum[:, 2 * hh + t:2 * hh + t + 1], None, ALU.mult)
                    last.then_inc(xpn_ready, 1)
                for hh in range(XH):
                    xh[0] += 1
                    dve.wait_ge(xhi_ready, layer_base(0, 24, l, xh[0]))
                    drain(tt(xlo[:, 2 * hh:2 * hh + 2, :], bank(f"xo_{hh}", 2, T), xhi[:, 2 * hh:2 * hh + 2, :], ALU.subtract))
                residual("xw", U_XO)
                normed(2, 6)
                split_lo(U_FF + 3)
                turned("n3", R_FN)
                for p in range(NP):
                    split_lo(unit_a(p) + 3)
                    dve.wait_ge(fconv_ready, layer_base(0, NP, l, p + 1))
                    y = fy[:, p % 2]
                    b = bank(f"fa{p}", 2, T)
                    for f in range(2):
                        c = RA + RB_W + 2 * p + f
                        ins = stt(y[:, f, 1:T], b[:, f, 0:T - 1], pcol[:, c:c + 1], y[:, f, 1:T], ALU.mult, ALU.add)
                    link(ins)
                    for f in range(2):
                        c = RA + RB_W + 44 + 2 * p + f
                        ins = stt(y[:, f, 0:T - 1], b[:, f, 1:T], pcol[:, c:c + 1], y[:, f, 0:T - 1], ALU.mult, ALU.add)
                    drain(ins)
                    split_lo(unit_a(p) + 4)
                    dve.wait_ge(gelu_ready, layer_base(0, NP, l, p + 1))
                    is_filled(dve, l, f"fg{p}")
                    drain(tt(fu[:, p % 2], bank(f"fg{p}", 2, T), y, ALU.mult))
                    dve.wait_ge(fhi_ready, layer_base(0, NP, l, p + 1))
                    tt(flo[:, p % 2], fu[:, p % 2], fhi[:, p % 2], ALU.subtract).then_inc(flo_ready, 1)
                split_lo(U)
                for i in range(4):
                    is_filled(dve, l, f"fd{i}")
                    n, t = i // 2, i % 2
                    hh = h[:, t, n * 512:(n + 1) * 512]
                    drain(tt(hh, hh, bank(f"fd{i}"), ALU.add))
                dve.sem_inc(dve_chain, CHAIN - chain[0])
            dve.wait_ge(gfin_in, 16)
            dve.wait_ge(mem_rstd, 2)
            for t in range(TT):
                ts(tmb[:, t, :], h[:, t, :], ss[:, 8 + t:9 + t], None, ALU.mult).then_inc(dve_pre, 1)
                dve.wait_ge(dve_pre, 2 + t)
                tt(tmb[:, t, :], tmb[:, t, :], memn[:, 0, :], ALU.mult).then_inc(fin_ready, 1)


_INS = ["x", "mem", "mix_norm_g", "w_in", "ml_conv_w", "ml_conv_b", "ml_gate_b", "ml_norm_g", "na_rpb", "gla_a_w2",
        "gla_a_b", "gla_norm_g", "w_out", "xattn_norm_g", "mem_norm_g", "w_xq", "w_xk", "w_xv", "w_xo", "ffn_norm_g",
        "w_up", "ffn_conv_w", "ffn_conv_b", "w_down", "final_norm_g"]


def kernel(**inputs):
    import concourse.bacc as bacc
    import numpy as np
    from concourse.bass_utils import run_bass_kernel_spmd

    nc = bacc.Bacc("TRN2", target_bir_lowering=False, num_devices=1, dynamic_dma_scratch_size=64)
    arrays, aps = {}, {}
    for name in _INS:
        v = np.ascontiguousarray(inputs[name])
        if name in ("x", "mem"):
            v = v[0]
        arrays[f"in_{name}"] = v
        aps[name] = nc.dram_tensor(f"in_{name}", v.shape, mybir.dt.from_np(v.dtype), kind="ExternalInput").ap()
    out = nc.dram_tensor("out", (T, DM), F32, kind="ExternalOutput").ap()
    build(nc, aps, out)
    r = run_bass_kernel_spmd(nc, [arrays], core_ids=[0])
    return r.results[0]["out"][None]
```

```python
from contextlib import ExitStack

import concourse.bass as bass
from concourse import mybir

F32 = mybir.dt.float32
F32R = mybir.dt.float32r
ALU = mybir.AluOpType
ACT = mybir.ActivationFunctionType
AX = mybir.AxisListType

P = 128
DM, T, DEPTH = 1024, 256, 2
GW, DH = 64, 64
MLH, NAH, GLH = 6, 5, 5
ML, NA, GK, GV = MLH * DH, NAH * DH, GLH * 32, GLH * DH
TT, KT = T // P, DM // P
RANK, LG = 16, 64
NCH = T // LG
XH, XD = 4, 256
FF = 2816
NP = FF // 256
EPS = 1e-6
NEG = -1e30
C_V, C_O, C_G = 2 * ML, 3 * ML, 4 * ML
C_NQ = C_G + 4 * MLH
C_NK, C_NV = C_NQ + NA, C_NQ + 2 * NA
C_GQ = C_NQ + 3 * NA
C_GK = C_GQ + GK
C_GV = C_GK + GK
C_GG = C_GV + GV
C_GA = C_GG + GV
COLS = C_GA + 2 * RANK

def stream():
    def fm(m, *columns):
        return (m, 0, KT, columns)

    def tm(m, c, n):
        return [(m, k, 4, ((c, n),)) for k in (0, 4)]

    u = [fm("w_in", (C_G, 32), (C_GQ + P, 32), (C_GK + P, 32), (C_GA, 32)), fm("w_in", (C_NQ + 256, DH), (C_NK + 256, DH))]
    u += [fm("w_in", (256 * i, 256)) for i in range(3)]
    u += tm("w_in", C_V, ML)
    u += [fm("w_in", (C_NQ, 256)), fm("w_in", (C_NK, 256)), fm("w_in", (C_GQ, P)), fm("w_in", (C_GK, P))]
    for c, n in ((C_NV, NA), (C_GV, GV), (C_O, ML), (C_GG, GV)):
        u += tm("w_in", c, n)
    u += [fm("w_xk", (256 * i, 256)) for i in range(4)]
    u += tm("w_xv", 0, 512) + tm("w_xv", 512, 512)
    u += tm("w_out", 0, 512) + tm("w_out", 512, 512)
    u += [fm("w_xq", (256 * i, 256)) for i in range(4)]
    u += tm("w_xo", 0, 512) + tm("w_xo", 512, 512)
    for p in range(NP):
        u += [fm("w_up", (256 * p, 256)), fm("w_up", (FF + 256 * p, 256))]
        if p:
            u.append(("w_down", 2 * p - 2, 2, ((0, DM),)))
    u.append(("w_down", 2 * NP - 2, 2, ((0, DM),)))
    return u

UNITS = stream()
U = len(UNITS)
WCOLS = [sum(n for _, n in cols) for _, _, _, cols in UNITS]
SIZE = [nk * w for (_, _, nk, _), w in zip(UNITS, WCOLS)]
RING = 3
UW = 2048
assert U % RING == 0
U_V, U_XV, U_WO, U_XQ, U_XO, U_FF = 5, 23, 27, 31, 35, 39
ML_FILL = ((7, ("nq",), (7,)), (8, ("nk",), (6,)), (9, ("gq",), (7,)), (10, ("gk",), (6,)),
           (11, ("nv0", "nv1"), (7, 6)), (13, ("gv0", "gv1"), (7, 6)))
NA_FILL = ((15, ("o0", "o1"), (7, 6)), (17, ("gg0", "gg1"), (7, 6)), (19, ("xk0",), (3,)), (20, ("xk1",), (7,)),
           (21, ("xk2",), (6,)), (22, ("xk3",), (7,)), None)
WIDTH = {"nv0": NA, "gv0": GV, "o0": ML, "gg0": GV}

def unit_a(p):
    return U_FF if p == 0 else U_FF + 2 + 3 * (p - 1)

def unit_d(p):
    return U - 1 if p == NP - 1 else U_FF + 4 + 3 * p

LANDS, SLOT_DMAS = [], [0] * RING
for _u in range(U):
    SLOT_DMAS[_u % RING] += len(UNITS[_u][3])
    LANDS.append(SLOT_DMAS[_u % RING])

def events():
    j = []

    def job(name, bank, by, unit=None):
        j.append((name, bank, by, unit))

    def tm(unit, names, banks, by):
        j.append((None, None, None, unit))
        job(names[0], banks[0], by)
        job(names[1], banks[1], by, unit + 1)

    def fill(f):
        if f and len(f[1]) == 2:
            tm(f[0], f[1], f[2], "A")
        elif f:
            job(f[1][0], f[2][0], "A", f[0])

    job("par", 7, "D")
    for i in range(4):
        job(f"n1_{i}", i, "D")
    job("mix", 4, "A", 0)
    job("nqk4", 5, "A", 1)
    job("gp", 6, "D")
    job("z0", 0, "A")
    job("z1", 1, "A")
    job("qk0", 7, "D", 2)
    job("qk1", 2, "D", 3)
    job("qk2", 3, "D", 4)
    tm(U_V, ("v0", "v1"), (4, 5), "A")
    job("gt", 6, "D")
    for h in range(MLH + 1):
        if h < MLH:
            job(f"mlb{h}", 2 + h % 2, "D")
            job(f"mls{h}", h % 2, "D")
        if h:
            job(f"mlo{h - 1}", 4 + (h - 1) % 2, "A")
        if h < MLH:
            fill(ML_FILL[h])
    for h in range(NAH + 2):
        if 1 <= h <= NAH:
            job(f"nat{h - 1}", 2 + (h - 1) % 2, "A")
        if h >= 2:
            job(f"nao{h - 2}", 4 + (h - 2) % 2, "D")
        if h == 2:
            for i in range(4):
                job(f"mt_{i}", (5, 7, 2, 1)[i], "D")
        if h < NAH:
            job(f"nas{h}", h % 2, "A")
        fill(NA_FILL[h])
    job("kt0", 5, "D")
    job("kt1", 6, "D")
    for n, b in (("ga", 0), ("kv", 4)):
        for i in range(4):
            job(f"{n}{i}", b + i, "D")
    tm(U_XV, ("xv0_0", "xv0_1"), (0, 1), "A")
    for i in range(4):
        job(f"go{i}", (2, 3, 0, 1)[i], "A")
    tm(U_XV + 2, ("xv1_0", "xv1_1"), (6, 7), "A")
    for i in range(4):
        job(f"mx_{i}", i, "D")
    for n in range(2):
        tm(U_WO + 2 * n, (f"wo{n}_0", f"wo{n}_1"), (4 + 2 * n, 5 + 2 * n), "D")
    for i in range(4):
        job(f"n2_{i}", i, "D")
    for i in range(4):
        job(f"xq{i}", 4 + i, "A", U_XQ + i)
    for n, b, by in (("xs", 0, "A"), ("xt", 4, "A"), ("xo_", 0, "D")):
        for i in range(XH):
            job(f"{n}{i}", b + i, by)
    for n in range(2):
        tm(U_XO + 2 * n, (f"xw{n}_0", f"xw{n}_1"), (4 + 2 * n, 5 + 2 * n), "D")
    for i in range(4):
        job(f"n3_{i}", i, "D")
    for p in range(NP + 1):
        if p < NP:
            job(f"fa{p}", 4 + 2 * (p % 2), "D", unit_a(p))
            job(f"fg{p}", 5 + 2 * (p % 2), "D", unit_a(p) + 1)
        if 0 < p < NP:
            j.append((None, None, None, unit_d(p - 1)))
    for i in range(4):
        job(f"fd{i}", i, "D", U - 1 if i == 3 else None)
    return j

EVENTS = events()
NE = len(EVENTS)
JOBS = [(n, b, d) for n, b, d, _ in EVENTS if n]
NJ = len(JOBS)
DONE = {n: i + 1 for i, (n, _, _, _) in enumerate(EVENTS) if n}
USED = {u: i + 1 for i, (_, _, _, u) in enumerate(EVENTS) if u is not None}
assert len(USED) == U
DRAINS = {e: [n for n, _, d in JOBS if d == e] for e in "AD"}
DRAIN = {n: (e, i + 1) for e in "AD" for i, n in enumerate(DRAINS[e])}
BANK = {n: b for n, b, _ in JOBS}

def before(name):
    i = [n for n, _, _ in JOBS].index(name)
    for k in range(1, NJ + 1):
        n, b, _ = JOBS[(i - k) % NJ]
        if b == BANK[name]:
            return n, k > i

R_MIX, R_XN, R_MN, R_FN, R_MG = 0, 8, 16, 24, 32
R_CW, R_CB, R_GB = 40, 58, 64
RA = 68
RB_W, RB_B, RB = 0, 66, 88
ARENA = 7960
CHAIN = 512


def build(nc, a, out):
    with ExitStack() as ctx:
        def sb(name, shape, dt=F32):
            return ctx.enter_context(nc.sbuf_tensor(name, shape, dt))

        def sem(name):
            return ctx.enter_context(nc.semaphore(name))

        raw = sb("raw", [P, RING, UW])
        whi = sb("whi", [P, RING, UW], F32R)
        wlo = sb("wlo", [P, RING, UW], F32R)
        h = sb("h", [P, TT, DM])
        tmb = sb("tmb", [P, TT, DM])
        memn = sb("memn", [P, TT, DM])
        xhi = sb("xhi", [P, KT, T], F32R)
        xlo = sb("xlo", [P, KT, T], F32R)
        spare = sb("spare", [P, 1])
        ss = sb("ss", [P, TT, 2])
        rt = sb("rt", [P, TT])
        dg = sb("dg", [P, TT, P])
        ident = sb("ident", [P, P])
        flip = sb("flip", [P, P])
        unit_row = sb("unit_row", [64, 64], F32R)
        ghi = sb("ghi", [64, T], F32R)
        glo = sb("glo", [64, T], F32R)
        ones = sb("ones", [P, T])
        mlm = sb("mlm", [P, 2, T])
        glm = sb("glm", [P, 2, TT, LG])
        bdm = sb("bdm", [P, 4, DH])
        reset = sb("reset", [P, 2 * T])
        win = sb("win", [P, GW])
        perm = sb("perm", [24, 2, 64])
        eps = sb("eps", [P, 1])
        rowa = sb("rowa", [RA, P])
        rowb = sb("rowb", [RB, P])
        pcol = sb("pcol", [P, RA + RB])
        gbias = sb("gbias", [24, 1])
        w2 = sb("w2", [P, 2, 256])
        bt = sb("bt", [P, NAH, 6, GW])
        with ExitStack() as early:
            qk = early.enter_context(nc.sbuf_tensor("qk", [P, 6, T], F32))
            naq = early.enter_context(nc.sbuf_tensor("naq", [P, 3, T], F32))
        fhi = sb("fhi", [P, 2, 2, T], F32R)
        flo = sb("flo", [P, 2, 2, T], F32R)
        sb("early_rest", [P, T])
        nak = sb("nak", [P, 3, T])
        mv = sb("mv", [P, TT, MLH, DH + 1])
        eo = sb("eo", [P, TT, ML])
        nav = sb("nav", [P, TT, NA])
        gv = sb("gv", [P, TT, GV])
        gg = sb("gg", [P, TT, GV])
        eg = sb("eg", [P, TT, GV])
        gq = sb("gq", [P, 2, T])
        gk = sb("gk", [P, 2, T])
        gaT = sb("gaT", [P, T])
        nmax = sb("nmax", [P, 2 * NAH])
        nsum = sb("nsum", [P, 2 * NAH])
        xk = sb("xk", [P, KT, T])
        xv = sb("xv", [P, TT, DM])
        gsb = sb("gsb", [24, T])
        gt = sb("gt", [P, TT, 2, 64])
        em = sb("em", [P, TT, 2, MLH])
        den = sb("den", [P, TT * 2 * MLH])
        hs = sb("hs", [P, 32])
        arena = sb("arena", [P, ARENA])
        used = [0]

        def carve(*shape, at=None, dt=None):
            n = 1
            for s in shape:
                n *= s
            o = used[0] if at is None else at
            used[0] = o + n
            assert used[0] <= ARENA
            v = arena[:, o:o + n]
            if dt:
                v = v.bitcast(dt)
            names = "abcde"[:len(shape)]
            if len(shape) == 1:
                return v
            return v.rearrange(f"p ({' '.join(names)}) -> p {' '.join(names)}", **dict(zip(names[1:], shape[1:])))

        qe = carve(6, T, at=0)
        E = carve(2, 768, at=0)
        PT = carve(2, 768)
        gI, gF, gE, gB, gA = (carve(T, at=3072 + i * T)[0:64, :] for i in range(5))
        hraw = carve(TT, 2, MLH, DH + 1, at=4352)
        zs = carve(4, T)
        np_ = carve(2, TT, T, at=5912)
        npt = carve(2, TT, TT, P)
        b1 = carve(4, T, at=0)
        b2 = carve(4, T)
        b3 = carve(4, T)
        b4 = carve(4, T)
        ktx = carve(2, TT, P)
        kty = carve(2, TT, 32)
        at = carve(GLH, 2, TT, LG)
        st = carve(2, 3, 320)
        xq = carve(KT, T, at=0)
        xp = carve(XH, TT, T)
        xpt = carve(XH, TT, T)
        fy = carve(2, 2, T, at=0)
        fu = carve(2, 2, T)
        zb = tmb[:, 0, :].rearrange("p (a b) -> p a b", b=T)
        zc = tmb[:, 1, :].rearrange("p (a b) -> p a b", b=T)
        mlh = qk[:, 0:3, :].rearrange("p a b -> p (a b)").rearrange("p (t h d) -> p t h d", t=TT, d=DH)
        sq = qk[:, 3:6, :].rearrange("p a b -> p (a b)").rearrange("p (t h d) -> p t h d", t=TT, d=DH)
        glh = bt[:, 0:2].rearrange("p a b c -> p (a b c)")[:, 0:640].rearrange("p (t h d) -> p t h d", t=TT, d=DH)
        glq = bt[:, 2:4].rearrange("p a b c -> p (a b c)")[:, 0:640].rearrange("p (t h d) -> p t h d", t=TT, d=DH)

        ps = [ctx.enter_context(nc.psum_tensor(f"bank{i}", [P, 512], F32)) for i in range(8)]

        def bank(name, *shape):
            v = ps[BANK[name]][:, :]
            if not shape:
                return v
            names = "abcd"[:len(shape)]
            return v.rearrange(f"p ({' '.join(names)}) -> p {' '.join(names)}", **dict(zip(names[1:], shape[1:])))

        landed = [sem(f"landed{i}") for i in range(RING)]
        hi_done = sem("hi_done")
        lo_done = sem("lo_done")
        te_done = sem("te_done")
        drained = {"A": sem("drained_act"), "D": sem("drained_dve")}
        const_ready = sem("const_ready")
        tok_in = sem("tok_in")
        mem_in = sem("mem_in")
        prm_in = sem("prm_in")
        gate_in = sem("gate_in")
        bt_in = sem("bt_in")
        rstd_ready = sem("rstd_ready")
        xn_ready = sem("xn_ready")
        xhi_ready = sem("xhi_ready")
        act_end = sem("act_end")
        dve_end = sem("dve_end")
        pool_chain = sem("pool_chain")
        gfin_in = sem("gfin_in")
        act_chain = sem("act_chain")
        dve_chain = sem("dve_chain")
        conv_ready = sem("conv_ready")
        tanh_ready = sem("tanh_ready")
        qk_ready = sem("qk_ready")
        gates_ready = sem("gates_ready")
        gln_ready = sem("gln_ready")
        scan_ready = sem("scan_ready")
        em_ready = sem("em_ready")
        e_ready = sem("e_ready")
        bias_ready = sem("bias_ready")
        nmax_ready = sem("nmax_ready")
        zb_ready = sem("zb_ready")
        zl_ready = sem("zl_ready")
        bc_ready = sem("bc_ready")
        eb_ready = sem("eb_ready")
        qd_ready = sem("qd_ready")
        state_ready = sem("state_ready")
        hsum_ready = sem("hsum_ready")
        hroot_ready = sem("hroot_ready")
        xmax_ready = sem("xmax_ready")
        xpn_ready = sem("xpn_ready")
        fconv_ready = sem("fconv_ready")
        gelu_ready = sem("gelu_ready")
        fhi_ready = sem("fhi_ready")
        flo_ready = sem("flo_ready")
        fin_ready = sem("fin_ready")
        stored = sem("stored")
        waited = sem("waited")

        prow = [(rowa, R_MIX, 8, P, lambda l: a["mix_norm_g"][bass.ds(l, 1), :].rearrange("o (r c) -> (o r) c", c=P)),
                (rowa, R_XN, 8, P, lambda l: a["xattn_norm_g"][bass.ds(l, 1), :].rearrange("o (r c) -> (o r) c", c=P)),
                (rowa, R_MN, 8, P, lambda l: a["mem_norm_g"][bass.ds(l, 1), :].rearrange("o (r c) -> (o r) c", c=P)),
                (rowa, R_FN, 8, P, lambda l: a["ffn_norm_g"][bass.ds(l, 1), :].rearrange("o (r c) -> (o r) c", c=P)),
                (rowa, R_MG, 3, P, lambda l: a["ml_norm_g"][bass.ds(l, 1), :].rearrange("o (r c) -> (o r) c", c=P)),
                (rowa, R_MG + 6, 2, P, lambda l: a["gla_norm_g"][bass.ds(l, 1), 64:320].rearrange("o (r c) -> (o r) c", c=P)),
                (rowa, R_CW, 18, P, lambda l: a["ml_conv_w"][bass.ds(l, 1)].rearrange("o w (r c) -> (o w r) c", c=P)),
                (rowa, R_CB, 6, P, lambda l: a["ml_conv_b"][bass.ds(l, 1)].rearrange("o (r c) -> (o r) c", c=P)),
                (rowb, RB_W, 66, P, lambda l: a["ffn_conv_w"][bass.ds(l, 1)].rearrange("o w (r c) -> (o w r) c", c=P)),
                (rowb, RB_B, 22, P, lambda l: a["ffn_conv_b"][bass.ds(l, 1)].rearrange("o (r c) -> (o r) c", c=P))]
        NPRM = len(prow) + 1 + 4

        def layer_base(pre, per, l, n):
            return l * per + (pre + n)

        def is_filled(eng, l, name):
            eng.wait_ge(te_done, layer_base(NE, NE, l, DONE[name]))

        def is_used(eng, l, u, back=False):
            eng.wait_ge(te_done, layer_base(0 if back else NE, NE, l, USED[u]))

        def slot_left(eng, l, u):
            is_used(eng, l, (u - RING) % U, u < RING)

        def is_drained(eng, l, name, back=False):
            e, i = DRAIN[name]
            n = len(DRAINS[e])
            eng.wait_ge(drained[e], layer_base(0 if back else n, n, l, i))

        def alone(eng):
            eng.sem_inc(waited, 1)

        block = ctx.enter_context(nc.Block())

        @block.sync
        def _(sp):
            for t in range(TT):
                sp.dma_start(h[:, t, :], a["x"][t * P:(t + 1) * P, :]).then_inc(tok_in, 16)
            with sp.Fori(0, DEPTH) as l:
                row = {m: sp.snap(l * a[m].shape[1]) for m in ("w_in", "w_xk", "w_down")}
                row["w_out"] = row["w_xv"] = row["w_xq"] = row["w_xo"] = row["w_up"] = row["w_xk"]
                row["w_in"] = row["w_xk"]
                lay = sp.snap(l * 1)

                def load(u):
                    sp.wait_ge(lo_done, layer_base(0, U, l, u + 1))
                    alone(sp)
                    m, k0, nk, cols = UNITS[u]
                    dst = raw[:, u % RING, 0:SIZE[u]].rearrange("p (k n) -> p k n", k=nk)
                    src = a[m][:, bass.ds(0, a[m].shape[1]), :].rearrange("l r c -> (l r) c")[bass.ds(row[m] + k0 * P, nk * P), :]
                    o = 0
                    for c, n in cols:
                        sp.dma_start(dst[:, :, o:o + n], src[:, c:c + n].rearrange("(k p) n -> p k n", p=P)).then_inc(landed[u % RING], 16)
                        o += n

                load(0)
                load(1)
                sp.wait_ge(const_ready, 1)
                sp.wait_ge(te_done, layer_base(0, NE, l, DONE["par"]))
                alone(sp)
                for tile, r, n, c, src in prow:
                    sp.dma_start(tile[r:r + n, 0:c], src(lay)).then_inc(prm_in, 16)
                sp.dma_start(rowa[R_MG + 5:R_MG + 6, 64:128], a["gla_norm_g"][bass.ds(lay, 1), 0:64]).then_inc(prm_in, 16)
                for z in range(2):
                    sp.dma_start(rowa[R_GB + 2 * z:R_GB + 2 * z + 1, :],
                                 a["gla_a_b"][bass.ds(lay, 1), z, 0:P]).then_inc(prm_in, 16)
                    sp.dma_start(rowa[R_GB + 2 * z + 1:R_GB + 2 * z + 2, 0:32],
                                 a["gla_a_b"][bass.ds(lay, 1), z, P:GK]).then_inc(prm_in, 16)
                sp.wait_ge(te_done, layer_base(0, NE, l, DONE["z1"]))
                sp.wait_ge(drained["A"], layer_base(0, len(DRAINS["A"]), l, DRAIN["mix"][1]))
                alone(sp)
                sp.dma_start(gbias[:, :], a["ml_gate_b"][bass.ds(lay, 1)].rearrange("o g k -> (o g k)").rearrange("(g k) -> g k", k=1)
                             ).then_inc(gate_in, 16)
                for z in range(2):
                    sp.dma_start(w2[96 + RANK * z:96 + RANK * (z + 1), z, 0:GK],
                                 a["gla_a_w2"][bass.ds(lay, 1), z].rearrange("o r k -> (o r) k")).then_inc(gate_in, 16)
                for u in range(2, U):
                    if u == 6:
                        sp.wait_ge(xn_ready, layer_base(0, 9, l, 5))
                        alone(sp)
                        for half in range(2):
                            for hh in range(NAH):
                                off = (hh * 15 + 5 - half) * 31 - 48
                                v = a["na_rpb"][bass.ds(lay, 1)]
                                src = bass.AP(v.tensor, v.offset + off, [[1, GW], [31, 6], [1, GW]])
                                sp.dma_start(bt[64 * half:64 * half + 64, hh], src).then_inc(bt_in, 16)
                    load(u)
            sp.wait_ge(te_done, NE * DEPTH + DONE["mt_3"])
            g = a["final_norm_g"]
            sp.dma_start(memn[:, 0, :], bass.AP(g.tensor, 0, [[0, P], [1, DM]])).then_inc(gfin_in, 16)
            for t in range(TT):
                sp.wait_ge(fin_ready, t + 1)
                sp.dma_start(out[t * P:(t + 1) * P, :], tmb[:, t, :]).then_inc(stored, 16)
            sp.wait_ge(stored, 16 * TT)

        @block.gpsimd
        def _(pool):
            g = nc.gpsimd
            n = [0]

            def step(ins):
                n[0] += 1
                ins.then_inc(pool_chain, 1)
                pool.wait_ge(pool_chain, n[0])

            def sel(v, op, fill, base, pat, cm):
                step(g.affine_select(out=v, in_=v, compare_op=op, fill=fill, base=base, pattern=pat, channel_multiplier=cm))

            for v, x in ((rowa, 1.0), (rowb, 1.0), (w2, 0.0), (eps, EPS), (ident, 0.0)):
                step(g.memset(v[:], x))
            sel(ident[:], ALU.not_equal, 1.0, 0, [[-1, P]], 1)
            pool.sem_inc(const_ready, 1)
            for v, x in ((flip, 0.0), (mlm, 0.0), (glm, 1.0), (bdm, 1.0), (win, 3e38),
                         (gq, 0.0), (gk, 0.0), (perm, 0.0), (ones, 1.0), (reset, 1.0), (mv, 1.0)):
                step(g.memset(v[:], x))
            sel(flip[:].rearrange("p (a c) -> p a c", a=2), ALU.not_equal, 1.0, 63, [[64, 2], [-1, 64]], -1)
            sel(mlm[:, 0, 0:P], ALU.is_ge, NEG, 0, [[1, P]], -1)
            sel(mlm[:, 1, P:T], ALU.is_ge, NEG, 0, [[-1, P]], 1)
            for half in range(2):
                q = slice(64 * half, 64 * half + 64)
                sel(glm[q, 0], ALU.is_ge, 0.0, 0, [[0, TT], [1, LG]], -1)
                sel(glm[q, 1], ALU.is_ge, 0.0, 0, [[0, TT], [-1, LG]], 1)
                sel(win[q, 0:48], ALU.is_ge, NEG, -63 + 8, [[1, 48]], 1)
                sel(win[q, 16:64], ALU.is_ge, NEG, 63 + 7 - 16, [[-1, 48]], -1)
            sel(bdm[:], ALU.is_ge, 0.0, 0, [[-32, 4], [0, DH]], 1)
            sel(bdm[:], ALU.is_ge, 0.0, 31, [[32, 4], [0, DH]], -1)
            for d in range(2):
                for kind in range(2):
                    sel(perm[:, kind, 32 * d:32 * d + MLH], ALU.not_equal, 1.0, -(12 * d + 6 * kind), [[-1, MLH]], 1)
            step(g.memset(reset[:].rearrange("p (c n) -> p c n", n=LG)[:, :, 0:1], 0.0))
            pool.sem_inc(const_ready, 1)

        @block.tensor
        def _(pe):
            mm = nc.tensor.matmul
            for s, n in ((lo_done, RING), (te_done, NE), (xn_ready, 9),
                         (drained["A"], len(DRAINS["A"])), (drained["D"], len(DRAINS["D"]))):
                pe.sem_inc(s, n)
            pe.wait_ge(const_ready, 1)
            with pe.Fori(0, DEPTH) as l:
                def free(name):
                    prev, back = before(name)
                    is_drained(pe, l, prev, back)

                def have(u):
                    pe.wait_ge(lo_done, layer_base(RING, U, l, u + 1))

                def split_mm(o, s_hi, s_lo, m_hi, m_lo, first, last):
                    mm(o, s_hi, m_hi, start=first, stop=False, skip_group_check=True)
                    mm(o, s_hi, m_lo, start=False, stop=False, skip_group_check=True)
                    return mm(o, s_lo, m_hi, start=False, stop=last, skip_group_check=True)

                def fm_unit(u, name, group=None):
                    free(name)
                    have(u)
                    hi = whi[:, u % RING, 0:SIZE[u]].rearrange("p (k n) -> p k n", k=KT)
                    lo = wlo[:, u % RING, 0:SIZE[u]].rearrange("p (k n) -> p k n", k=KT)
                    for f in range(WCOLS[u] // P):
                        for k in range(KT):
                            if group and f == 0 and k % 2 == 0:
                                xt_ready(f"{group}_{k // 2}")
                            cs = slice(f * P, f * P + P)
                            last = split_mm(bank(name, 2, T)[:, f, :], hi[:, k, cs], lo[:, k, cs], xhi[:, k, :], xlo[:, k, :],
                                            k == 0, k == KT - 1)
                    last.then_inc(te_done, 1)

                def tm_units(u, names, n, group=None):
                    for half in range(2):
                        have(u + half)
                        for t in range(TT):
                            if half == 0:
                                free(names[t])
                            hi = whi[:, (u + half) % RING, 0:4 * n].rearrange("p (k n) -> p k n", k=4)
                            lo = wlo[:, (u + half) % RING, 0:4 * n].rearrange("p (k n) -> p k n", k=4)
                            for k in range(4):
                                kk = 4 * half + k
                                if group and t == 0 and kk % 2 == 0:
                                    xt_ready(f"{group}_{kk // 2}")
                                s = slice(t * P, t * P + P)
                                last = split_mm(bank(names[t])[:, 0:n], xhi[:, kk, s], xlo[:, kk, s],
                                                hi[:, k, :], lo[:, k, :], kk == 0, kk == KT - 1)
                            if half or t:
                                last.then_inc(te_done, 1)

                def fill(f):
                    if f and len(f[1]) == 2:
                        tm_units(f[0], f[1], WIDTH[f[1][0]])
                    elif f:
                        fm_unit(f[0], f[1][0], "mt" if f[1][0] == "xk0" else None)

                def turn(group, src, first, between=None):
                    last_drain = {}
                    for i in range(4):
                        prev, back = before(f"{group}_{i}")
                        e, n = DRAIN[prev]
                        last_drain[e] = max(last_drain.get(e, (0, "", False)), (n, prev, back))
                    assert len({b for _, _, b in last_drain.values()}) == 1
                    for n, prev, back in last_drain.values():
                        is_drained(pe, l, prev, back)
                    for t in range(TT):
                        pe.wait_ge(xn_ready, layer_base(9, 9, l, first + t))
                        for k in range(KT):
                            last = mm(bank(f"{group}_{k // 2}", 2, T)[:, k % 2, t * P:(t + 1) * P],
                                      src[:, t, k * P:(k + 1) * P], dg[:, t, :], start=True, stop=True)
                            if t == TT - 1 and k % 2:
                                last.then_inc(te_done, 1)
                        if between and t == 0:
                            between()

                def xt_ready(name):
                    is_drained(pe, l, name)

                def parameters():
                    pe.wait_ge(prm_in, layer_base(0, 16 * NPRM, l, 16 * NPRM))
                    free("par")
                    nc.tensor.transpose(bank("par")[:, 0:RA], rowa[:, :], ident[0:RA, 0:RA])
                    nc.tensor.transpose(bank("par")[:, P:P + RB], rowb[:, :], ident[0:RB, 0:RB]).then_inc(te_done, 1)

                turn("n1", h, 1, parameters)
                fm_unit(0, "mix", "n1")
                fm_unit(1, "nqk4")
                pe.wait_ge(const_ready, 2)
                free("gp")
                is_drained(pe, l, "mix")
                mm(bank("gp")[0:64, 0:T], perm[:, 0, :], gsb[:, :], start=True, stop=True)
                mm(bank("gp")[0:64, T:2 * T], perm[:, 1, :], gsb[:, :], start=True, stop=True).then_inc(te_done, 1)
                pe.wait_ge(gate_in, layer_base(0, 16 * 3, l, 16 * 3))
                for z in range(2):
                    free(f"z{z}")
                    for d in range(2):
                        last = mm(bank(f"z{z}", 2, T)[:, d, :], w2[96:128, d, P * z:P * z + P], gaT[96:128, :], start=True, stop=True)
                    last.then_inc(te_done, 1)
                fm_unit(2, "qk0")
                fm_unit(3, "qk1")
                fm_unit(4, "qk2")
                tm_units(U_V, ("v0", "v1"), ML)
                free("gt")
                pe.wait_ge(scan_ready, layer_base(0, 1, l, 1))
                alone(pe)
                for t in range(TT):
                    nc.tensor.transpose(bank("gt", 4, P)[:, 2 * t, 0:64], gI[:, t * P:(t + 1) * P], ident[0:64, 0:64])
                    last = nc.tensor.transpose(bank("gt", 4, P)[:, 2 * t + 1, 0:64], gB[:, t * P:(t + 1) * P], ident[0:64, 0:64])
                last.then_inc(te_done, 1)
                pe.wait_ge(qk_ready, layer_base(0, 3, l, 3))
                for hh in range(MLH + 1):
                    if hh < MLH:
                        free(f"mlb{hh}")
                        for d in range(2):
                            q = 32 * d + hh
                            pick = unit_row[:, q:q + 1].broadcast_to([64, P])
                            mm(bank(f"mlb{hh}", 2, T)[:, d, :], pick, ghi[:, :], start=True, stop=False)
                            last = mm(bank(f"mlb{hh}", 2, T)[:, d, :], pick, glo[:, :], start=False, stop=True)
                        last.then_inc(te_done, 1)
                        r, j = slice(64 * (hh % 2), 64 * (hh % 2) + 64), hh // 2
                        free(f"mls{hh}")
                        for jt in range(TT):
                            last = mm(bank(f"mls{hh}", TT, T)[:, jt, :], qk[r, 3 + j, jt * P:(jt + 1) * P], qk[r, j, :], start=True, stop=True)
                        last.then_inc(te_done, 1)
                    if hh:
                        g = hh - 1
                        is_drained(pe, l, f"mls{g}")
                        free(f"mlo{g}")
                        w = PT[:, g % 2, :]
                        o = bank(f"mlo{g}")[:, 0:4 * 65].rearrange("p (t d e) -> p t d e", t=TT, d=2)
                        for t, d, src in ((0, 0, ((0, 0),)), (1, 0, ((0, 128), (1, 256))),
                                          (0, 1, ((0, 384), (1, 512))), (1, 1, ((1, 640),))):
                            for i, (jt, c) in enumerate(src):
                                last = mm(o[:, t, d, :], w[:, c:c + P], mv[:, jt, g, :], start=i == 0, stop=i == len(src) - 1)
                        last.then_inc(te_done, 1)
                    if hh < MLH:
                        fill(ML_FILL[hh])
                pe.wait_ge(bias_ready, layer_base(0, 1, l, 1))
                is_drained(pe, l, "nk")
                for hh in range(NAH + 2):
                    if 1 <= hh <= NAH:
                        g = hh - 1
                        is_drained(pe, l, f"nas{g}")
                        free(f"nat{g}")
                        for t in range(TT):
                            for jt in range(TT):
                                last = nc.tensor.transpose(bank(f"nat{g}", TT, TT, P)[:, t, jt, :], np_[:, g % 2, t, jt * P:(jt + 1) * P], ident[:])
                        last.then_inc(te_done, 1)
                    if hh >= 2:
                        g = hh - 2
                        is_drained(pe, l, f"nat{g}")
                        free(f"nao{g}")
                        for t in range(TT):
                            for jt in range(TT):
                                last = mm(bank(f"nao{g}")[:, t * DH:(t + 1) * DH], npt[:, g % 2, t, jt, :],
                                          nav[:, jt, g * DH:(g + 1) * DH], start=jt == 0, stop=jt == 1)
                        last.then_inc(te_done, 1)
                    if hh == 2:
                        turn("mt", memn, 3)
                    if hh < NAH:
                        r, j = slice(64 * (hh % 2), 64 * (hh % 2) + 64), hh // 2
                        free(f"nas{hh}")
                        for t in range(TT):
                            o = bank(f"nas{hh}", TT, T)[:, t, :]
                            b = bt[:, hh, 2 - 2 * t:6 - 2 * t, :].rearrange("p a b -> p (a b)")
                            mm(o, flip[:], b, start=True, stop=False)
                            last = mm(o, naq[r, j, t * P:(t + 1) * P], nak[r, j, :], start=False, stop=True)
                        last.then_inc(te_done, 1)
                    fill(NA_FILL[hh])
                pe.wait_ge(qd_ready, layer_base(0, 1, l, 1))
                free("kt0")
                free("kt1")
                for d in range(2):
                    for t in range(TT):
                        last = nc.tensor.transpose(bank("kt0", 2, TT, P)[:, d, t, :], b4[:, d * 2, t * P:(t + 1) * P], ident[:])
                last.then_inc(te_done, 1)
                for d in range(2):
                    for t in range(TT):
                        last = nc.tensor.transpose(bank("kt1", 4, P)[:, 2 * d + t, 0:32], b4[0:32, d * 2 + 1, t * P:(t + 1) * P], ident[0:32, 0:32])
                last.then_inc(te_done, 1)
                for i in range(4):
                    free(f"ga{i}")
                    for hh in ([0, 4] if i == 0 else [i]):
                        lane, r = (0, slice(32 * hh, 32 * hh + 32)) if hh < 4 else (1, slice(0, 32))
                        for d in range(2):
                            for c in range(NCH):
                                q = slice(64 * (c % 2), 64 * (c % 2) + 64)
                                cc = slice(c * LG, c * LG + LG)
                                last = mm(bank(f"ga{i}", 2, 2, TT, LG)[q, hh // 4, d, c // 2, :], b3[r, 2 * d + lane, cc], b2[r, 2 * d + lane, cc],
                                          start=True, stop=True, skip_group_check=True)
                    last.then_inc(te_done, 1)
                is_drained(pe, l, "kt1")
                for i, lst in enumerate((((0, 0), (0, 2)), ((0, 1), (1, 3)), ((1, 2),), ((1, 1),))):
                    free(f"kv{i}")
                    n = 0
                    for d, c in lst:
                        q = slice(64 * (c % 2), 64 * (c % 2) + 64)
                        last = mm(bank(f"kv{i}", 2, T)[:, n, :], ktx[q, d, c // 2, :], gv[q, c // 2, 0:256], start=True, stop=True, skip_group_check=True)
                        n += 1
                    if i >= 2:
                        for n, (d, c) in enumerate((((0, 0), (0, 2), (1, 2)), ((0, 1), (1, 3), (1, 1)))[i - 2]):
                            q = slice(64 * (c % 2), 64 * (c % 2) + 64)
                            last = mm(bank(f"kv{i}")[0:32, 256 + n * 64:320 + n * 64], kty[q, d, c // 2, :], gv[q, c // 2, 256:320],
                                      start=True, stop=True, skip_group_check=True)
                    last.then_inc(te_done, 1)
                tm_units(U_XV, ("xv0_0", "xv0_1"), 512)
                is_drained(pe, l, "ga3")
                pe.wait_ge(state_ready, layer_base(0, 1, l, 1))
                for i in range(4):
                    t, par = i // 2, i % 2
                    c = 2 * t + par
                    q = slice(64 * par, 64 * par + 64)
                    cc = slice(c * LG, c * LG + LG)
                    free(f"go{i}")
                    o = bank(f"go{i}")
                    first = True
                    for d in range(2):
                        n = c if d == 0 else NCH - 1 - c
                        if n:
                            mm(o[q, 0:256], b2[:, 2 * d, cc], st[:, d, n - 1, 0:256], start=first, stop=False, skip_group_check=True)
                            mm(o[q, 256:320], b2[0:32, 2 * d + 1, cc], st[0:32, d, n - 1, 256:320], start=False, stop=False, skip_group_check=True)
                            first = False
                    for d in range(2):
                        for hh in range(GLH):
                            last = mm(o[q, hh * DH:(hh + 1) * DH], at[q, hh, d, t, :], gv[q, t, hh * DH:(hh + 1) * DH],
                                      start=False, stop=d == 1, skip_group_check=True)
                    last.then_inc(te_done, 1)
                tm_units(U_XV + 2, ("xv1_0", "xv1_1"), 512)
                pe.wait_ge(xn_ready, layer_base(9, 9, l, 5))
                for i in range(4):
                    free(f"mx_{i}")
                    for kk in range(2):
                        for t in range(TT):
                            last = nc.tensor.transpose(bank(f"mx_{i}", 2, T)[:, kk, t * P:(t + 1) * P],
                                                       tmb[:, t, (2 * i + kk) * P:(2 * i + kk + 1) * P], ident[:])
                    last.then_inc(te_done, 1)
                for n in range(2):
                    tm_units(U_WO + 2 * n, (f"wo{n}_0", f"wo{n}_1"), 512, None if n else "mx")
                turn("n2", h, 6)
                for i in range(4):
                    fm_unit(U_XQ + i, f"xq{i}", None if i else "n2")
                for hh in range(XH):
                    is_drained(pe, l, f"xq{hh}")
                    free(f"xs{hh}")
                    for t in range(TT):
                        for kk in range(2):
                            last = mm(bank(f"xs{hh}", TT, T)[:, t, :], xq[:, 2 * hh + kk, t * P:(t + 1) * P], xk[:, 2 * hh + kk, :],
                                      start=kk == 0, stop=kk == 1)
                    last.then_inc(te_done, 1)
                for hh in range(XH):
                    pe.wait_ge(xpn_ready, layer_base(0, XH, l, hh + 1))
                    free(f"xt{hh}")
                    for t in range(TT):
                        for jt in range(TT):
                            last = nc.tensor.transpose(bank(f"xt{hh}", TT, T)[:, jt, t * P:(t + 1) * P], xp[:, hh, t, jt * P:(jt + 1) * P], ident[:])
                    last.then_inc(te_done, 1)
                for hh in range(XH):
                    is_drained(pe, l, f"xt{hh}")
                    free(f"xo_{hh}")
                    for f in range(2):
                        for jt in range(TT):
                            last = mm(bank(f"xo_{hh}", 2, T)[:, f, :], xv[:, jt, hh * XD + f * P:hh * XD + (f + 1) * P], xpt[:, hh, jt, :],
                                      start=jt == 0, stop=jt == 1)
                    last.then_inc(te_done, 1)
                for n in range(2):
                    tm_units(U_XO + 2 * n, (f"xw{n}_0", f"xw{n}_1"), 512, None if n else "xo")
                turn("n3", h, 8)
                for p in range(NP + 1):
                    if p < NP:
                        fm_unit(unit_a(p), f"fa{p}", None if p else "n3")
                        fm_unit(unit_a(p) + 1, f"fg{p}")
                    if p:
                        g = p - 1
                        u = unit_d(g)
                        have(u)
                        pe.wait_ge(flo_ready, layer_base(0, NP, l, g + 1))
                        hi = whi[:, u % RING, :].rearrange("p (k n) -> p k n", k=2)
                        lo = wlo[:, u % RING, :].rearrange("p (k n) -> p k n", k=2)
                        for n in range(2):
                            for t in range(TT):
                                if g == 0:
                                    free(f"fd{2 * n + t}")
                                for k in range(2):
                                    s = slice(t * P, t * P + P)
                                    last = split_mm(bank(f"fd{2 * n + t}"), fhi[:, g % 2, k, s], flo[:, g % 2, k, s],
                                                    hi[:, k, n * 512:(n + 1) * 512], lo[:, k, n * 512:(n + 1) * 512],
                                                    g == 0 and k == 0, g == NP - 1 and k == 1)
                                if g == NP - 1 or (n, t) == (1, 1):
                                    last.then_inc(te_done, 1)

        @block.scalar
        def _(act):
            A = nc.scalar.activation
            def square(src, n, t):
                c = slice(512 * n, 512 * n + 512)
                return A(tmb[:, t, c], src[:, t, c], ACT.Square, accum_out=ss[:, t, n:n + 1])

            def table(f):
                A(spare[:, :], eps[:, :], f)

            def mean_part(t):
                return A(ss[:, t, 0:1], ss[:, t, 0:1], ACT.Identity, scale=1.0 / DM, bias=eps[:, :])

            def root(t):
                return A(rt[:, t:t + 1], ss[:, t, 1:2], ACT.Sqrt, scale=1.0 / DM, bias=ss[:, t, 0:1])

            def rms(src, ready, link):
                for n in range(2):
                    for t in range(TT):
                        ready(n, t)
                        link(square(src, n, t))
                        if n:
                            root(t).then_inc(rstd_ready, 1)
                        else:
                            link(mean_part(t))

            act.wait_ge(const_ready, 1)
            for t in range(TT):
                act.dma_start(memn[:, t, :], a["mem"][t * P:(t + 1) * P, :]).then_inc(mem_in, 16)
            with act.Fori(0, DEPTH) as l:
                chain = [0]

                def link(ins):
                    chain[0] += 1
                    ins.then_inc(act_chain, 1)
                    act.wait_ge(act_chain, layer_base(0, CHAIN, l, chain[0]))

                nhi = [0]

                def split_hi(upto):
                    while nhi[0] < min(upto, U):
                        u = nhi[0]
                        act.wait_ge(landed[u % RING], layer_base(0, 16 * SLOT_DMAS[u % RING], l, 16 * LANDS[u]))
                        slot_left(act, l, u)
                        n = SIZE[u]
                        A(whi[:, u % RING, 0:n], raw[:, u % RING, 0:n], ACT.Copy).then_inc(hi_done, 1)
                        nhi[0] += 1

                def turned(group, gcol, n=4):
                    for i in range(n):
                        is_filled(act, l, f"{group}_{i}")
                        for kk in range(2):
                            k = 2 * i + kk
                            last = A(xhi[:, k, :], bank(f"{group}_{i}", 2, T)[:, kk, :], ACT.Copy, scale=pcol[:, gcol + k:gcol + k + 1])
                        last.then_inc(xhi_ready, 1)

                def drain(ins):
                    ins.then_inc(drained["A"], 1)

                def fill(f):
                    if not f:
                        return
                    for i, nm in enumerate(f[1]):
                        split_hi(f[0] + i + 3)
                        is_filled(act, l, nm)
                        b = bank(nm)
                        b2T = bank(nm, 2, T)
                        t = int(nm[-1]) if len(f[1]) == 2 else 0
                        if nm == "gq":
                            drain(A(gq[:, 0, :], b2T[:, 0, :], ACT.Copy, scale=32 ** -0.5))
                        elif nm == "gk":
                            drain(A(gk[:, 0, :], b2T[:, 0, :], ACT.Copy))
                        elif nm == "nq":
                            drain(A(naq[:, 0:2, :], b2T, ACT.Copy, scale=DH ** -0.5))
                        elif nm == "nk":
                            drain(A(nak[:, 0:2, :], b2T, ACT.Copy))
                        elif nm[:2] == "xk":
                            j = int(nm[2])
                            drain(A(xk[:, 2 * j:2 * j + 2, :], b2T, ACT.Copy))
                        elif nm[0] == "o":
                            drain(A(eo[:, t, :], b[:, 0:ML], ACT.Tanh, scale=0.5))
                        elif nm[:2] == "gg":
                            A(gg[:, t, :], b[:, 0:GV], ACT.Copy)
                            drain(A(eg[:, t, :], b[:, 0:GV], ACT.Tanh, scale=0.5))
                        else:
                            drain(A((nav if nm[:2] == "nv" else gv)[:, t, :], b[:, 0:GV], ACT.Copy))

                table(ACT.Sqrt)
                act.wait_ge(tok_in, 16 * TT)
                rms(h, lambda n, t: is_drained(act, l, f"fd{2 * n + t}", True), link)
                split_hi(1)
                is_drained(act, l, "par")
                turned("n1", R_MIX)
                split_hi(3)
                act.wait_ge(const_ready, 2)
                act.wait_ge(gate_in, layer_base(0, 16 * 3, l, 16 * 3))
                is_filled(act, l, "mix")
                b = bank("mix")
                A(gsb[:, :], b[0:24, 0:T], ACT.Identity, bias=gbias[:, :])
                A(gaT[96:128, :], b[96:128, 0:T], ACT.Copy)
                A(gq[0:32, 1, :], b[32:64, 0:T], ACT.Copy, scale=32 ** -0.5)
                drain(A(gk[0:32, 1, :], b[64:96, 0:T], ACT.Copy))
                split_hi(4)
                is_filled(act, l, "nqk4")
                b = bank("nqk4")
                A(naq[0:64, 2, :], b[0:64, 0:T], ACT.Copy, scale=DH ** -0.5)
                drain(A(nak[0:64, 2, :], b[64:128, 0:T], ACT.Copy))
                for z in range(2):
                    is_filled(act, l, f"z{z}")
                    for d in range(2):
                        last = A(zs[:, 2 * d + z, :], bank(f"z{z}", 2, T)[:, d, :], ACT.Identity,
                                 bias=pcol[:, R_GB + 2 * d + z:R_GB + 2 * d + z + 1])
                    drain(last)
                for i in range(3):
                    split_hi(5 + i)
                    is_filled(act, l, f"qk{i}")
                    for f in range(2):
                        j = 2 * i + f
                        last = A(qk[:, j, :], bank(f"qk{i}", 2, T)[:, f, :], ACT.Identity,
                                 scale=pcol[:, R_CW + 6 + j:R_CW + 7 + j], bias=pcol[:, R_CB + j:R_CB + j + 1])
                    last.then_inc(conv_ready, 1)
                    if i == 0:
                        split_hi(6)
                        act.wait_ge(gates_ready, layer_base(0, 1, l, 1))
                        A(gE[:, :], gE[:, :], ACT.Exp)
                        act.wait_ge(zb_ready, layer_base(0, 1, l, 1))
                        link(A(zb, zb, ACT.Exp))
                        A(gE[:, :], gE[:, :], ACT.Ln, bias=ones[0:64, 0:1]).then_inc(gln_ready, 1)
                        A(zb, zb, ACT.Ln, bias=ones[:, 0:1]).then_inc(zl_ready, 1)
                split_hi(8)
                for i in range(3):
                    is_drained(act, l, f"qk{i}")
                    A(qe[:, 2 * i:2 * i + 2, :], qk[:, 2 * i:2 * i + 2, :], ACT.Tanh, scale=0.5).then_inc(tanh_ready, 1)
                for t in range(TT):
                    split_hi(U_V + t + 3)
                    is_filled(act, l, f"v{t}")
                    drain(A(mv[:, t, :, 0:DH], bank(f"v{t}")[:, 0:ML].rearrange("p (h d) -> p h d", d=DH), ACT.Copy))
                split_hi(U_V + 5)
                is_drained(act, l, "gt")
                for d in range(2):
                    last = A(em[:, :, d, :], gt[:, :, 1, 32 * d:32 * d + MLH], ACT.Exp, scale=-1.0)
                last.then_inc(em_ready, 1)
                for hh in range(MLH + 1):
                    if hh < MLH:
                        is_drained(act, l, f"mlb{hh}")
                        A(E[:, hh % 2, :], E[:, hh % 2, :], ACT.Exp).then_inc(e_ready, 1)
                    if hh:
                        g = hh - 1
                        is_filled(act, l, f"mlo{g}")
                        drain(A(hraw[:, :, :, g, :], bank(f"mlo{g}")[:, 0:260].rearrange("p (t d e) -> p t d e", t=TT, d=2), ACT.Copy))
                    if hh < MLH:
                        fill(ML_FILL[hh])
                act.wait_ge(bc_ready, layer_base(0, 1, l, 1))
                A(b1[:], zc, ACT.Exp, scale=1.0 / 16).then_inc(eb_ready, 1)
                A(b3[:], zc, ACT.Exp, scale=-1.0 / 16).then_inc(eb_ready, 1)
                for hh in range(NAH + 2):
                    if 1 <= hh <= NAH:
                        is_filled(act, l, f"nat{hh - 1}")
                        drain(A(npt[:, (hh - 1) % 2].rearrange("p a b c -> p (a b c)"), bank(f"nat{hh - 1}"), ACT.Copy))
                    if hh == 2:
                        turned("mt", R_MN)
                    if hh < NAH:
                        act.wait_ge(nmax_ready, layer_base(0, NAH, l, hh + 1))
                        for t in range(TT):
                            last = A(np_[:, hh % 2, t, :], bank(f"nas{hh}", TT, T)[:, t, :], ACT.Exp,
                                     bias=nmax[:, 2 * hh + t:2 * hh + t + 1], accum_out=nsum[:, 2 * hh + t:2 * hh + t + 1])
                        drain(last)
                    fill(NA_FILL[hh])
                    if hh == 0:
                        act.wait_ge(mem_in, 16 * TT)
                        rms(memn, lambda n, t: None, link)

                def head_root(v, i):
                    act.wait_ge(hsum_ready, layer_base(0, 2, l, i))
                    A(v, v, ACT.Sqrt, scale=1.0 / DH, bias=eps[:, :]).then_inc(hroot_ready, 1)

                head_root(hs[:, 0:12], 1)
                for t in range(TT):
                    split_hi(U_XV + t + 3)
                    is_filled(act, l, f"xv0_{t}")
                    drain(A(xv[:, t, 0:512], bank(f"xv0_{t}"), ACT.Copy))
                for i in range(4):
                    is_filled(act, l, f"go{i}")
                    q = slice(64 * (i % 2), 64 * (i % 2) + 64)
                    drain(A(glh[q, i // 2].rearrange("p h d -> p (h d)"), bank(f"go{i}")[q, 0:GV], ACT.Copy))
                split_hi(U_XV + 2 + 3)
                head_root(hs[:, 12:22], 2)
                for t in range(TT):
                    split_hi(U_XV + 2 + t + 3)
                    is_filled(act, l, f"xv1_{t}")
                    drain(A(xv[:, t, 512:1024], bank(f"xv1_{t}"), ACT.Copy))
                turned("mx", R_MG)
                split_hi(U_WO + 3)

                def added(name, u):
                    def ready(n, t):
                        split_hi(u + min(2 * n + t + 3, 5))
                        is_drained(act, l, f"{name}{n}_{t}")
                    return ready

                rms(h, added("wo", U_WO), link)
                turned("n2", R_XN)
                for i in range(4):
                    split_hi(U_XQ + i + 3)
                    if i == 0:
                        table(ACT.Exp)
                    is_filled(act, l, f"xq{i}")
                    drain(A(xq[:, 2 * i:2 * i + 2, :], bank(f"xq{i}", 2, T), ACT.Copy, scale=XD ** -0.5))
                for hh in range(XH):
                    act.wait_ge(xmax_ready, layer_base(0, XH, l, hh + 1))
                    for t in range(TT):
                        last = A(xp[:, hh, t, :], bank(f"xs{hh}", TT, T)[:, t, :], ACT.Exp,
                                 bias=nmax[:, 2 * hh + t:2 * hh + t + 1], accum_out=nsum[:, 2 * hh + t:2 * hh + t + 1])
                    drain(last)
                table(ACT.Sqrt)
                for hh in range(XH):
                    is_filled(act, l, f"xt{hh}")
                    drain(A(xpt[:, hh].rearrange("p a b -> p (a b)"), bank(f"xt{hh}"), ACT.Copy))
                for hh in range(XH):
                    is_filled(act, l, f"xo_{hh}")
                    A(xhi[:, 2 * hh:2 * hh + 2, :], bank(f"xo_{hh}", 2, T), ACT.Copy).then_inc(xhi_ready, 1)
                rms(h, added("xw", U_XO), link)
                turned("n3", R_FN)
                for p in range(NP):
                    split_hi(unit_a(p) + 3)
                    is_filled(act, l, f"fa{p}")
                    for f in range(2):
                        j = 2 * p + f
                        last = A(fy[:, p % 2, f, :], bank(f"fa{p}", 2, T)[:, f, :], ACT.Identity,
                                 scale=pcol[:, RA + RB_W + 22 + j:RA + RB_W + 23 + j], bias=pcol[:, RA + RB_B + j:RA + RB_B + j + 1])
                    last.then_inc(fconv_ready, 1)
                    split_hi(unit_a(p) + 4)
                    is_drained(act, l, f"fa{p}")
                    A(fy[:, p % 2], fy[:, p % 2], ACT.Gelu_apprx_tanh).then_inc(gelu_ready, 1)
                    is_drained(act, l, f"fg{p}")
                    A(fhi[:, p % 2], fu[:, p % 2], ACT.Copy).then_inc(fhi_ready, 1)
                split_hi(U)
                act.sem_inc(act_chain, CHAIN - chain[0])

            n_end = [0]

            def end_link(ins):
                n_end[0] += 1
                ins.then_inc(act_end, 1)
                act.wait_ge(act_end, n_end[0])

            table(ACT.Sqrt)
            rms(h, lambda n, t: is_drained(act, DEPTH - 1, f"fd{2 * n + t}"), end_link)

        @block.vector
        def _(dve):
            V = nc.vector
            ts, tt, stt = V.tensor_scalar, V.tensor_tensor, V.scalar_tensor_tensor
            dve.wait_ge(const_ready, 1)
            V.tensor_copy(unit_row[:, :], ident[0:64, 0:64])
            dve.wait_ge(tok_in, 16 * TT)
            with dve.Fori(0, DEPTH) as l:
                chain = [0]

                def link(ins):
                    chain[0] += 1
                    ins.then_inc(dve_chain, 1)
                    dve.wait_ge(dve_chain, layer_base(0, CHAIN, l, chain[0]))

                nlo = [0]

                def split_lo(upto):
                    while nlo[0] < min(upto, U):
                        u = nlo[0]
                        dve.wait_ge(hi_done, layer_base(0, U, l, u + 1))
                        n = SIZE[u]
                        tt(wlo[:, u % RING, 0:n], raw[:, u % RING, 0:n], whi[:, u % RING, 0:n], ALU.subtract).then_inc(lo_done, 1)
                        nlo[0] += 1

                def drain(ins):
                    ins.then_inc(drained["D"], 1)

                def normed(i):
                    for t in range(TT):
                        dve.wait_ge(rstd_ready, layer_base(0, 8, l, 2 * i + t + 1))
                        link(V.reciprocal(rt[:, t:t + 1], rt[:, t:t + 1]))
                        ts(dg[:, t, :], ident[:], rt[:, t:t + 1], None, ALU.mult).then_inc(xn_ready, 1)

                xh = [0]

                def turned(group, gcol):
                    for i in range(4):
                        xh[0] += 1
                        dve.wait_ge(xhi_ready, layer_base(0, 24, l, xh[0]))
                        for kk in range(2):
                            k = 2 * i + kk
                            last = stt(xlo[:, k, :], bank(f"{group}_{i}", 2, T)[:, kk, :], pcol[:, gcol + k:gcol + k + 1], xhi[:, k, :],
                                       ALU.mult, ALU.subtract)
                        drain(last)

                def residual(name, u):
                    for n in range(2):
                        for t in range(TT):
                            split_lo(u + min(2 * n + t + 3, 5))
                            is_filled(dve, l, f"{name}{n}_{t}")
                            hh = h[:, t, n * 512:(n + 1) * 512]
                            last = tt(hh, hh, bank(f"{name}{n}_{t}"), ALU.add)
                            drain(last)
                    is_drained(dve, l, f"{name}1_1")

                normed(0)
                split_lo(1)
                is_filled(dve, l, "par")
                V.tensor_copy(pcol[:, 0:RA], bank("par")[:, 0:RA])
                drain(V.tensor_copy(pcol[:, RA:RA + RB], bank("par")[:, P:P + RB]))
                turned("n1", R_MIX)
                split_lo(3)
                dve.wait_ge(const_ready, 2)
                split_lo(4)
                is_filled(dve, l, "gp")
                V.tensor_copy(gI[:, :], bank("gp")[0:64, 0:T])
                drain(V.tensor_copy(gF[:, :], bank("gp")[0:64, T:2 * T]))
                is_drained(dve, l, "gp")
                stt(gE[:, :], gF[:, :], -1.0, gF[:, :], ALU.mult, ALU.min).then_inc(gates_ready, 1)
                split_lo(5)
                is_drained(dve, l, "z1")
                stt(zb, zs[:], -1.0, zs[:], ALU.mult, ALU.min).then_inc(zb_ready, 1)
                for i in range(3):
                    split_lo(5 + i)
                    dve.wait_ge(conv_ready, layer_base(0, 3, l, i + 1))
                    y = qk[:, 2 * i:2 * i + 2, :]
                    b = bank(f"qk{i}", 2, T)
                    for f in range(2):
                        j = 2 * i + f
                        ins = stt(y[:, f, 1:T], b[:, f, 0:T - 1], pcol[:, R_CW + j:R_CW + j + 1], y[:, f, 1:T], ALU.mult, ALU.add)
                    link(ins)
                    for f in range(2):
                        j = 2 * i + f
                        ins = stt(y[:, f, 0:T - 1], b[:, f, 1:T], pcol[:, R_CW + 12 + j:R_CW + 13 + j], y[:, f, 0:T - 1], ALU.mult, ALU.add)
                    drain(ins)
                    if i == 0:
                        split_lo(6)
                        dve.wait_ge(gln_ready, layer_base(0, 1, l, 1))
                        link(stt(gF[:, :], gF[:, :], 0.0, gE[:, :], ALU.min, ALU.subtract))
                        V.tensor_tensor_scan(gB[0:32, :], ones[0:32, :], gF[0:32, :], 0.0, ALU.mult, ALU.add)
                        link(V.tensor_tensor_scan(gB[32:64, ::-1], ones[32:64, :], gF[32:64, ::-1], 0.0, ALU.mult, ALU.add))
                        link(tt(gI[:, :], gI[:, :], gB[:, :], ALU.subtract))
                        V.tensor_tensor_scan(gA[0:32, :], gI[0:32, :], gI[0:32, :], 0.0, ALU.max, ALU.max)
                        link(V.tensor_tensor_scan(gA[32:64, ::-1], gI[32:64, ::-1], gI[32:64, ::-1], 0.0, ALU.max, ALU.max))
                        link(tt(gB[:, :], gB[:, :], gA[:, :], ALU.add))
                        link(ts(gA[:, :], gA[:, :], -1.0, None, ALU.mult))
                        link(V.tensor_copy(ghi[:, :], gA[:, :]))
                        tt(glo[:, :], gA[:, :], ghi[:, :], ALU.subtract).then_inc(scan_ready, 1)
                for i in range(3):
                    dve.wait_ge(tanh_ready, layer_base(0, 3, l, i + 1))
                    y = qk[:, 2 * i:2 * i + 2, :]
                    stt(y, qe[:, 2 * i:2 * i + 2, :], 1.0, y, ALU.add, ALU.mult).then_inc(qk_ready, 1)
                split_lo(8)
                is_filled(dve, l, "gt")
                V.tensor_copy(gt[:].rearrange("p t k c -> p (t k) c"), bank("gt", 4, P)[:, :, 0:64]).then_inc(drained["D"], 1)
                is_drained(dve, l, "gt")
                for hh in range(MLH):
                    is_filled(dve, l, f"mlb{hh}")
                    nb = bank(f"mlb{hh}", 2, T)
                    e, w = E[:, hh % 2, :], PT[:, hh % 2, :]

                    def aj(t, d):
                        return gt[:, t, 0, 32 * d + hh:32 * d + hh + 1]

                    stt(e[:, 0:256], nb[:, 0, :], aj(0, 0), mlm[:, 0, :], ALU.add, ALU.min)
                    stt(e[:, 256:384], nb[:, 0, P:T], aj(1, 0), mlm[:, 0, 0:P], ALU.add, ALU.min)
                    stt(e[:, 384:512], nb[:, 1, 0:P], aj(0, 1), mlm[:, 1, P:T], ALU.add, ALU.min)
                    drain(stt(e[:, 512:768], nb[:, 1, :], aj(1, 1), mlm[:, 1, :], ALU.add, ALU.min))
                    split_lo(ML_FILL[hh][0] + (3 if hh else 2))
                    if hh == 4:
                        dve.wait_ge(bt_in, layer_base(0, 16 * 2 * NAH, l, 16 * 2 * NAH))
                        bv = bt[:].rearrange("p a b c -> p (a b) c")
                        tt(bv, bv, win[:].rearrange("p (o c) -> p o c", o=1).broadcast_to([P, 6 * NAH, GW]), ALU.min).then_inc(bias_ready, 1)
                    dve.wait_ge(e_ready, layer_base(0, MLH, l, hh + 1))
                    is_filled(dve, l, f"mls{hh}")
                    s = bank(f"mls{hh}", TT, T)
                    sc = DH ** -0.5 / 4
                    stt(w[:, 0:256], s[:, 0, :], sc, e[:, 0:256], ALU.mult, ALU.mult)
                    stt(w[:, 256:384], s[:, 1, P:T], sc, e[:, 256:384], ALU.mult, ALU.mult)
                    stt(w[:, 384:512], s[:, 0, 0:P], sc, e[:, 384:512], ALU.mult, ALU.mult)
                    drain(stt(w[:, 512:768], s[:, 1, :], sc, e[:, 512:768], ALU.mult, ALU.mult))
                    if hh == 0:
                        dve.wait_ge(zl_ready, layer_base(0, 1, l, 1))
                        link(stt(zs[:], zs[:], 0.0, zb, ALU.min, ALU.subtract))
                        la = zs[:].rearrange("p a b -> p (a b)")
                        bc = tmb[:, 1, :]
                        V.tensor_tensor_scan(bc[:, 0:512], reset[:], la[:, 0:512], 0.0, ALU.mult, ALU.add)
                        V.tensor_tensor_scan(bc[:, 1023:511:-1], reset[:], la[:, 1023:511:-1], 0.0, ALU.mult, ALU.add).then_inc(bc_ready, 1)
                    split_lo(ML_FILL[hh][0] + 2 + len(ML_FILL[hh][1]))

                def head_squares(v, squares, n, nh):
                    link(tt(squares, v, v, ALU.mult))
                    V.reduce_sum(hs[:, n:n + 2 * nh].rearrange("p (t h) -> p t h", t=TT), squares, AX.X).then_inc(hsum_ready, 1)

                def scaled(v, n, c, width, gate, i, gain):
                    dve.wait_ge(hroot_ready, layer_base(0, 2, l, i))
                    nh = width // DH
                    s = hs[:, n:n + 2 * nh]
                    link(V.reciprocal(s, s))
                    link(ts(s, s, 0.5, None, ALU.mult))
                    s = s.rearrange("p (t h o) -> p t h o", t=TT, o=1)
                    for t in range(TT):
                        ins = tt(v[:, t], v[:, t], s[:, t].broadcast_to([P, nh, DH]), ALU.mult)
                    link(ins)
                    return stt(tmb[:, :, c:c + width], gate[:], gain, v.rearrange("p t h d -> p t (h d)"), ALU.add, ALU.mult)

                for hh in range(NAH + 2):
                    if hh >= 2:
                        g = hh - 2
                        is_drained(dve, l, f"nas{g}")
                        link(V.reciprocal(nsum[:, 2 * g:2 * g + 2], nsum[:, 2 * g:2 * g + 2]))
                        is_filled(dve, l, f"nao{g}")
                        for t in range(TT):
                            last = ts(tmb[:, t, ML + g * DH:ML + (g + 1) * DH], bank(f"nao{g}")[:, t * DH:(t + 1) * DH],
                                      nsum[:, 2 * g + t:2 * g + t + 1], None, ALU.mult)
                        drain(last)
                    if hh == 2:
                        turned("mt", R_MN)
                    if hh < NAH:
                        is_filled(dve, l, f"nas{hh}")
                        V.tensor_reduce(nmax[:, 2 * hh:2 * hh + 2], bank(f"nas{hh}", TT, T), AX.X, ALU.max, negate=True).then_inc(nmax_ready, 1)
                    if hh == 1:
                        normed(1)
                    if NA_FILL[hh]:
                        split_lo(NA_FILL[hh][0] + 3)
                    if hh == 0:
                        is_drained(dve, l, f"mlo{MLH - 1}")
                        dve.wait_ge(em_ready, layer_base(0, 1, l, 1))
                        hr = hraw[:].rearrange("p t d h e -> p (t d h) e")
                        link(stt(den[:, :], hr[:, :, DH], -1.0, hr[:, :, DH], ALU.mult, ALU.max))
                        link(tt(den[:, :], den[:, :], em[:].rearrange("p t d h -> p (t d h)"), ALU.max))
                        link(V.reciprocal(den[:, :], den[:, :]))
                        link(tt(hr[:, :, 0:DH], hr[:, :, 0:DH], den[:].rearrange("p (n o) -> p n o", o=1).broadcast_to([P, 24, DH]), ALU.mult))
                        link(tt(mlh, hraw[:, :, 0, :, 0:DH], hraw[:, :, 1, :, 0:DH], ALU.add))
                    if hh == 2:
                        dve.wait_ge(eb_ready, layer_base(0, 2, l, 2))
                        is_drained(dve, l, "gk")
                        for d in range(2):
                            tt(b2[:, 2 * d:2 * d + 2, :], gq[:], b1[:, 2 * d:2 * d + 2, :], ALU.mult)
                            ins = tt(b3[:, 2 * d:2 * d + 2, :], gk[:], b3[:, 2 * d:2 * d + 2, :], ALU.mult)
                        link(ins)
                    if hh == 3:
                        for d in range(2):
                            cv = lambda v: v[:, 2 * d:2 * d + 2, :].rearrange("p a (c n) -> p (a c) n", n=LG)
                            e = cv(b1)[:, :, (LG - 1) * (1 - d):(LG - 1) * (1 - d) + 1]
                            last = tt(cv(b4), cv(b3), e.broadcast_to([P, 2 * NCH, LG]), ALU.mult)
                        last.then_inc(qd_ready, 1)
                    if hh == 4:
                        head_squares(mlh, sq, 0, MLH)
                    if hh == 0:
                        split_lo(NA_FILL[hh][0] + 4)
                is_filled(dve, l, "kt0")
                drain(V.tensor_copy(ktx[:].rearrange("p a b c -> p (a b c)"), bank("kt0")))
                is_filled(dve, l, "kt1")
                drain(V.tensor_copy(kty[:].rearrange("p a b c -> p (a b) c"), bank("kt1", 4, P)[:, :, 0:32]))
                for i in range(4):
                    is_filled(dve, l, f"ga{i}")
                    for hh in ([4, 0] if i == 0 else [i]):
                        last = tt(at[:, hh].rearrange("p a b c -> p (a b c)"), bank(f"ga{i}", 2, T)[:, hh // 4, :],
                                  glm[:].rearrange("p a b c -> p (a b c)"), ALU.mult)
                    drain(last)
                split_lo(U_XV + 3)
                scaled(mlh, 0, 0, ML, eo, 1, 1.0)
                link(stt(gg[:], eg[:], 1.0, gg[:], ALU.add, ALU.mult))
                for i in range(4):
                    is_filled(dve, l, f"kv{i}")
                bd = bdm[:].rearrange("p a b -> p (a b)")
                where = {(0, 0): ("kv0", 0, "kv2", 0), (0, 2): ("kv0", 1, "kv2", 1), (0, 1): ("kv1", 0, "kv3", 0),
                         (1, 3): ("kv1", 1, "kv3", 1), (1, 2): ("kv2", 0, "kv2", 2), (1, 1): ("kv3", 0, "kv3", 2)}
                for d in range(2):
                    for n in range(3):
                        c = n if d == 0 else NCH - 1 - n
                        jx, ix, jy, iy = where[d, c]
                        tt(st[:, d, n, 0:256], bank(jx, 2, T)[:, ix, :], bd, ALU.mult)
                        ins = V.tensor_copy(st[0:32, d, n, 256:320], bank(jy)[0:32, 256 + 64 * iy:320 + 64 * iy])
                link(ins)
                dve.sem_inc(drained["D"], 4)
                for n in range(1, 3):
                    for d in range(2):
                        c = n if d == 0 else NCH - 1 - n
                        e = c * LG + (LG - 1) * (1 - d)
                        stt(st[:, d, n, 0:256], st[:, d, n - 1, 0:256], b1[:, 2 * d, e:e + 1], st[:, d, n, 0:256], ALU.mult, ALU.add)
                        ins = stt(st[0:32, d, n, 256:320], st[0:32, d, n - 1, 256:320], b1[0:32, 2 * d + 1, e:e + 1],
                                  st[0:32, d, n, 256:320], ALU.mult, ALU.add)
                    if n == 1:
                        link(ins)
                ins.then_inc(state_ready, 1)

                split_lo(U_XV + 4)
                is_drained(dve, l, "go3")
                split_lo(U_XV + 2 + 3)
                head_squares(glh, glq, 12, GLH)
                scaled(glh, 12, ML + NA, GV, gg, 2, 0.0).then_inc(xn_ready, 1)
                turned("mx", R_MG)
                split_lo(U_WO + 3)
                residual("wo", U_WO)
                normed(2)
                turned("n2", R_XN)
                split_lo(U_XQ + 3)
                for i in range(4):
                    split_lo(U_XQ + i + 3)
                for hh in range(XH + 1):
                    if hh < XH:
                        is_filled(dve, l, f"xs{hh}")
                        V.tensor_reduce(nmax[:, 2 * hh:2 * hh + 2], bank(f"xs{hh}", TT, T), AX.X, ALU.max, negate=True).then_inc(xmax_ready, 1)
                    if hh:
                        g = hh - 1
                        is_drained(dve, l, f"xs{g}")
                        link(V.reciprocal(nsum[:, 2 * g:2 * g + 2], nsum[:, 2 * g:2 * g + 2]))
                        for t in range(TT):
                            last = ts(xp[:, g, t, :], xp[:, g, t, :], nsum[:, 2 * g + t:2 * g + t + 1], None, ALU.mult)
                        last.then_inc(xpn_ready, 1)
                for hh in range(XH):
                    xh[0] += 1
                    dve.wait_ge(xhi_ready, layer_base(0, 24, l, xh[0]))
                    drain(tt(xlo[:, 2 * hh:2 * hh + 2, :], bank(f"xo_{hh}", 2, T), xhi[:, 2 * hh:2 * hh + 2, :], ALU.subtract))
                residual("xw", U_XO)
                normed(3)
                turned("n3", R_FN)
                split_lo(U_FF + 3)
                for p in range(NP):
                    split_lo(unit_a(p) + 3)
                    dve.wait_ge(fconv_ready, layer_base(0, NP, l, p + 1))
                    y = fy[:, p % 2]
                    b = bank(f"fa{p}", 2, T)
                    for f in range(2):
                        c = RA + RB_W + 2 * p + f
                        ins = stt(y[:, f, 1:T], b[:, f, 0:T - 1], pcol[:, c:c + 1], y[:, f, 1:T], ALU.mult, ALU.add)
                    link(ins)
                    for f in range(2):
                        c = RA + RB_W + 44 + 2 * p + f
                        ins = stt(y[:, f, 0:T - 1], b[:, f, 1:T], pcol[:, c:c + 1], y[:, f, 0:T - 1], ALU.mult, ALU.add)
                    drain(ins)
                    split_lo(unit_a(p) + 4)
                    dve.wait_ge(gelu_ready, layer_base(0, NP, l, p + 1))
                    is_filled(dve, l, f"fg{p}")
                    drain(tt(fu[:, p % 2], bank(f"fg{p}", 2, T), y, ALU.mult))
                    dve.wait_ge(fhi_ready, layer_base(0, NP, l, p + 1))
                    tt(flo[:, p % 2], fu[:, p % 2], fhi[:, p % 2], ALU.subtract).then_inc(flo_ready, 1)
                split_lo(U)
                for i in range(4):
                    is_filled(dve, l, f"fd{i}")
                    n, t = i // 2, i % 2
                    hh = h[:, t, n * 512:(n + 1) * 512]
                    drain(tt(hh, hh, bank(f"fd{i}"), ALU.add))
                dve.sem_inc(dve_chain, CHAIN - chain[0])
            dve.wait_ge(gfin_in, 16)
            for t in range(TT):
                dve.wait_ge(rstd_ready, 8 * DEPTH + t + 1)
                V.reciprocal(rt[:, t:t + 1], rt[:, t:t + 1]).then_inc(dve_end, 1)
                dve.wait_ge(dve_end, t + 1)
                stt(tmb[:, t, :], h[:, t, :], rt[:, t:t + 1], memn[:, 0, :], ALU.mult, ALU.mult).then_inc(fin_ready, 1)


_INS = ["x", "mem", "mix_norm_g", "w_in", "ml_conv_w", "ml_conv_b", "ml_gate_b", "ml_norm_g", "na_rpb", "gla_a_w2",
        "gla_a_b", "gla_norm_g", "w_out", "xattn_norm_g", "mem_norm_g", "w_xq", "w_xk", "w_xv", "w_xo", "ffn_norm_g",
        "w_up", "ffn_conv_w", "ffn_conv_b", "w_down", "final_norm_g"]


def kernel(**inputs):
    import concourse.bacc as bacc
    import numpy as np
    from concourse.bass_utils import run_bass_kernel_spmd

    nc = bacc.Bacc("TRN2", target_bir_lowering=False, num_devices=1, dynamic_dma_scratch_size=64)
    arrays, aps = {}, {}
    for name in _INS:
        v = np.ascontiguousarray(inputs[name])
        if name in ("x", "mem"):
            v = v[0]
        arrays[f"in_{name}"] = v
        aps[name] = nc.dram_tensor(f"in_{name}", v.shape, mybir.dt.from_np(v.dtype), kind="ExternalInput").ap()
    out = nc.dram_tensor("out", (T, DM), F32, kind="ExternalOutput").ap()
    build(nc, aps, out)
    r = run_bass_kernel_spmd(nc, [arrays], core_ids=[0])
    return r.results[0]["out"][None]
```
